# Optimizing a Trainium2 kernel written in Bass

```python
import math
import jax, jax.numpy as jnp
from jax import lax
import numpy as np

D_MODEL = 2048
BATCH = 1
SEQ = 512
DEPTH = 1

HEAD_DIM = 128
MIX_WIDTH = D_MODEL
N_RET_HEADS = MIX_WIDTH // HEAD_DIM // 2
N_DIFF_HEADS = MIX_WIDTH // HEAD_DIM // 2
RET_DK = HEAD_DIM
RET_DV = HEAD_DIM
RET_WIDTH = N_RET_HEADS * RET_DV
DIFF_DQK = HEAD_DIM // 2
DIFF_DV = HEAD_DIM
DIFF_WIDTH = N_DIFF_HEADS * DIFF_DV
D_FF = 4 * D_MODEL
RET_CHUNK = 128
Q_BLOCK = 128
ROPE_THETA = 500000.0
RET_THETA = 10000.0
DIFF_ROT_DIM = DIFF_DQK // 4
NORM_EPS = 1e-6
GN_EPS = 1e-5
IN_SPLITS = (RET_WIDTH, RET_WIDTH, RET_WIDTH, RET_WIDTH,
             N_DIFF_HEADS * 2 * DIFF_DQK, N_DIFF_HEADS * 2 * DIFF_DQK, DIFF_WIDTH)
IN_WIDTH = sum(IN_SPLITS)

kernel_name = "hybrid_retention_diffattn_block"

def lambda_init(layer_idx):
    return 0.8 - 0.6 * math.exp(-0.3 * layer_idx)

def rms_norm(x, w, eps=NORM_EPS):
    xf = x.astype(jnp.float32)
    y = xf * lax.rsqrt(jnp.mean(xf * xf, axis=-1, keepdims=True) + eps)
    return (y * w.astype(jnp.float32)).astype(x.dtype)

def modulate(h, shift, scale):
    return h * (1.0 + scale[:, None, :]) + shift[:, None, :]

def rotary(x, rot_dim, base):
    T = x.shape[-2]
    pos = jnp.arange(T, dtype=jnp.float32)
    inv = base ** (-jnp.arange(0, rot_dim, 2, dtype=jnp.float32) / rot_dim)
    ang = pos[:, None] * inv[None, :]
    cos = jnp.cos(ang).astype(x.dtype)
    sin = jnp.sin(ang).astype(x.dtype)
    half = rot_dim // 2
    x1 = x[..., :half]
    x2 = x[..., half:rot_dim]
    return jnp.concatenate([x1 * cos - x2 * sin, x2 * cos + x1 * sin, x[..., rot_dim:]], axis=-1)

def retention_chunkwise(q, k, v, log_gamma):
    B, H, T, dk = q.shape
    dv = v.shape[-1]
    C = RET_CHUNK
    NC = T // C
    idx = jnp.arange(C, dtype=jnp.float32)
    rel = idx[:, None] - idx[None, :]
    lg = log_gamma[:, None, None]
    decay = jnp.where(rel[None] >= 0, jnp.exp(jnp.maximum(rel, 0.0)[None] * lg), 0.0)
    xi = jnp.exp((idx + 1.0)[None, :] * log_gamma[:, None])
    zeta = jnp.exp((C - 1.0 - idx)[None, :] * log_gamma[:, None])
    chunk_decay = jnp.exp(C * log_gamma)

    def to_chunks(t):
        return t.reshape(B, H, NC, C, t.shape[-1]).transpose(2, 0, 1, 3, 4)

    def step(S, inp):
        qc, kc, vc = inp
        inner = jnp.einsum('bhid,bhjd->bhij', qc, kc) * decay[None]
        o = jnp.einsum('bhij,bhjv->bhiv', inner, vc)
        o = o + jnp.einsum('bhid,bhdv->bhiv', qc, S) * xi[None, :, :, None]
        S = S * chunk_decay[None, :, None, None] + jnp.einsum(
            'bhjd,bhjv->bhdv', kc * zeta[None, :, :, None], vc)
        return S, o

    S0 = jnp.zeros((B, H, dk, dv), jnp.float32)
    _, o = lax.scan(step, S0, (to_chunks(q), to_chunks(k), to_chunks(v)))
    return o.transpose(1, 2, 0, 3, 4).reshape(B, H, T, dv)

def diff_attention(q, k, v, lam):
    T = q.shape[3]
    nb = T // Q_BLOCK
    scale = DIFF_DQK ** -0.5
    kpos = jnp.arange(T)

    def block(i):
        qb = lax.dynamic_slice_in_dim(q, i * Q_BLOCK, Q_BLOCK, axis=3)
        s = jnp.einsum('bhcqd,bhckd->bhcqk', qb, k) * scale
        qpos = i * Q_BLOCK + jnp.arange(Q_BLOCK)
        mask = kpos[None, :] <= qpos[:, None]
        s = jnp.where(mask, s, -jnp.inf)
        p = jax.nn.softmax(s, axis=-1)
        a = p[:, :, 0] - lam * p[:, :, 1]
        return jnp.einsum('bhqk,bhkd->bhqd', a, v)

    o = lax.map(block, jnp.arange(nb))
    B, H = q.shape[0], q.shape[1]
    return o.transpose(1, 2, 0, 3, 4).reshape(B, H, T, v.shape[-1])

def setup_inputs(seed: int = 0) -> dict:
    key = jax.random.key(seed)
    ks = jax.random.split(key, 18)
    f32 = jnp.float32
    x = jax.random.normal(ks[0], (BATCH, SEQ, D_MODEL), f32)
    c = jax.random.normal(ks[1], (BATCH, D_MODEL), f32)
    w_ada = jax.random.normal(ks[2], (DEPTH, D_MODEL, 6 * D_MODEL), f32) * (0.5 * D_MODEL ** -0.5)
    b_ada = jax.random.normal(ks[3], (DEPTH, 6 * D_MODEL), f32) * 0.02
    norm1_w = 1.0 + 0.05 * jax.random.normal(ks[4], (DEPTH, D_MODEL), f32)
    norm2_w = 1.0 + 0.05 * jax.random.normal(ks[5], (DEPTH, D_MODEL), f32)
    w_in = jax.random.normal(ks[6], (DEPTH, D_MODEL, IN_WIDTH), f32) * D_MODEL ** -0.5
    ret_gn_w = 1.0 + 0.05 * jax.random.normal(ks[7], (DEPTH, RET_WIDTH), f32)
    diff_lq1 = 0.1 * jax.random.normal(ks[8], (DEPTH, DIFF_DQK), f32)
    diff_lk1 = 0.1 * jax.random.normal(ks[9], (DEPTH, DIFF_DQK), f32)
    diff_lq2 = 0.1 * jax.random.normal(ks[10], (DEPTH, DIFF_DQK), f32)
    diff_lk2 = 0.1 * jax.random.normal(ks[11], (DEPTH, DIFF_DQK), f32)
    diff_subln_w = 1.0 + 0.05 * jax.random.normal(ks[12], (DEPTH, DIFF_WIDTH), f32)
    w_out = jax.random.normal(ks[13], (DEPTH, MIX_WIDTH, D_MODEL), f32) * MIX_WIDTH ** -0.5
    w_mlp1 = jax.random.normal(ks[14], (DEPTH, D_MODEL, D_FF), f32) * D_MODEL ** -0.5
    w_mlp2 = jax.random.normal(ks[15], (DEPTH, D_FF, D_MODEL), f32) * D_FF ** -0.5
    final_norm_w = 1.0 + 0.05 * jax.random.normal(ks[16], (D_MODEL,), f32)
    return {"x": x, "c": c, "w_ada": w_ada, "b_ada": b_ada, "norm1_w": norm1_w,
            "norm2_w": norm2_w, "w_in": w_in, "ret_gn_w": ret_gn_w,
            "diff_lq1": diff_lq1, "diff_lk1": diff_lk1, "diff_lq2": diff_lq2,
            "diff_lk2": diff_lk2, "diff_subln_w": diff_subln_w, "w_out": w_out,
            "w_mlp1": w_mlp1, "w_mlp2": w_mlp2, "final_norm_w": final_norm_w}

def reference(x, c, w_ada, b_ada, norm1_w, norm2_w, w_in, ret_gn_w, diff_lq1, diff_lk1,
              diff_lq2, diff_lk2, diff_subln_w, w_out, w_mlp1, w_mlp2, final_norm_w):
    B, T, _ = x.shape
    f32 = jnp.float32
    log_gamma = jnp.log(1.0 - 2.0 ** (-5.0 - jnp.arange(N_RET_HEADS, dtype=f32)))
    split_pts = list(np.cumsum(IN_SPLITS)[:-1])
    silu_c = jax.nn.silu(c)

    for l in range(DEPTH):
        mod = silu_c @ w_ada[l] + b_ada[l]
        sh1, sc1, g1, sh2, sc2, g2 = jnp.split(mod, 6, axis=-1)

        h = modulate(rms_norm(x, norm1_w[l]), sh1, sc1)
        proj = h @ w_in[l]
        rq, rk, rv, rg, dq, dk, dv = jnp.split(proj, split_pts, axis=-1)

        def heads(t, d):
            return t.reshape(B, T, -1, d).transpose(0, 2, 1, 3).astype(f32)
        rq_h = rotary(heads(rq, RET_DK), RET_DK, RET_THETA)
        rk_h = rotary(heads(rk, RET_DK), RET_DK, RET_THETA) * (RET_DK ** -0.5)
        rv_h = heads(rv, RET_DV)
        y_ret = retention_chunkwise(rq_h, rk_h, rv_h, log_gamma)
        mu = jnp.mean(y_ret, axis=-1, keepdims=True)
        var = jnp.mean(jnp.square(y_ret - mu), axis=-1, keepdims=True)
        y_ret = (y_ret - mu) * lax.rsqrt(var + GN_EPS)
        y_ret = y_ret.transpose(0, 2, 1, 3).reshape(B, T, RET_WIDTH) * ret_gn_w[l].astype(f32)
        y_ret = y_ret * jax.nn.silu(rg.astype(f32))

        dq_h = dq.reshape(B, T, N_DIFF_HEADS, 2, DIFF_DQK).transpose(0, 2, 3, 1, 4).astype(f32)
        dk_h = dk.reshape(B, T, N_DIFF_HEADS, 2, DIFF_DQK).transpose(0, 2, 3, 1, 4).astype(f32)
        dq_h = rotary(dq_h, DIFF_ROT_DIM, ROPE_THETA)
        dk_h = rotary(dk_h, DIFF_ROT_DIM, ROPE_THETA)
        dv_h = heads(dv, DIFF_DV)
        lam_init = lambda_init(l)
        lam = (jnp.exp(jnp.sum(diff_lq1[l].astype(f32) * diff_lk1[l].astype(f32)))
               - jnp.exp(jnp.sum(diff_lq2[l].astype(f32) * diff_lk2[l].astype(f32)))
               + lam_init)
        y_dif = diff_attention(dq_h, dk_h, dv_h, lam)
        y_dif = y_dif * lax.rsqrt(jnp.mean(y_dif * y_dif, axis=-1, keepdims=True) + GN_EPS)
        y_dif = y_dif.transpose(0, 2, 1, 3).reshape(B, T, DIFF_WIDTH)
        y_dif = y_dif * diff_subln_w[l].astype(f32) * (1.0 - lam_init)

        mixed = jnp.concatenate([y_ret, y_dif], axis=-1).astype(x.dtype) @ w_out[l]
        x = x + g1[:, None, :] * mixed

        h2 = modulate(rms_norm(x, norm2_w[l]), sh2, sc2)
        mlp = jnp.square(jax.nn.relu(h2 @ w_mlp1[l])) @ w_mlp2[l]
        x = x + g2[:, None, :] * mlp

    return rms_norm(x, final_norm_w)


_drawn_inputs = setup_inputs


def setup_inputs(seed=0):
    import zlib

    import numpy as np

    out = dict(_drawn_inputs(seed))
    spreads = {}
    factors = {'norm1_w': 3.733,
     'ret_gn_w': 8.0,
     'diff_lq1': 5.977,
     'diff_lk1': 64.0,
     'diff_lq2': 64.0,
     'diff_subln_w': 32.2,
     'norm2_w': 8.0,
     'diff_lk2': 8.0}
    for name, (base, spread) in spreads.items():
        noise = np.random.default_rng([zlib.crc32(name.encode()), seed]).standard_normal(out[name].shape)
        drawn = base * np.exp(spread * noise) if base else spread * noise
        out[name] = __import__('jax').numpy.asarray(drawn.astype(out[name].dtype))
    for name, factor in factors.items():
        out[name] = (out[name] * factor).astype(out[name].dtype)
    return out
```

```python
from contextlib import ExitStack

import numpy as np

import concourse.bass as bass
from concourse import mybir

F32 = mybir.dt.float32
F32R = mybir.dt.float32r
BF16 = mybir.dt.bfloat16
ALU = mybir.AluOpType
ACT = mybir.ActivationFunctionType
AX_X = mybir.AxisListType.X

P128 = 128
D = 2048
TOK = 512
KT = D // P128
TB = TOK // P128
HD = 128
NRET = 8
NDIF = 8
DQK = HD // 2
FF = 4 * D
HALF = D // 2
NORM_EPS = 1e-6
GN_EPS = 1e-5
LAM_INIT = 0.8 - 0.6
QK_SCALE = float(DQK) ** -0.5
BIG = 3.0e38
SQUARE_TOP = 1.8446e19
MEAN_TOP = 2.658e36

LN_SCALE = 2.0 ** -64

BLOCKS = 8
CHUNK = BLOCKS * P128
NRAW = 4
NW = 2
NADA = 4
MLP_GROUPS = FF // P128 // BLOCKS

C_DIF = 8 * NRET
C_OUT = C_DIF + 6 * NDIF
C_MLP = C_OUT + 2 * KT
PER_GROUP = 4 * BLOCKS
N_CHUNKS = C_MLP + PER_GROUP * MLP_GROUPS
A_RET = 4 * KT
N_ADA = 12 * KT

STRIP = [0, 512, 896, 1152]
STRIPS = 1280
ROWS = [0, 128, 384, 768]

V_B1, V_B, V_N1, V_N2, V_FIN, V_HEAD = 0, 32, 96, 112, 128, 144
N_VEC = 160


class Count:

    def __init__(self, base, *terms):
        self.base, self.terms = base, terms

    def __add__(self, n):
        return Count(self.base + n, *self.terms)

    def value(self, per=1, add=0):
        total = self.base // per + add
        for factor, register in self.terms:
            assert factor % per == 0
            total = (factor // per) * register + total
        return total

    def place(self, ring):
        assert all(factor % ring == 0 for factor, _ in self.terms)
        return self.base % ring

    def above(self, n):
        return bool(self.terms) or self.base >= n


def block_kernel(nc, x_t, c, ada, weights, vecs, lams, rot, decay, ident_in, mask_in, out):
    with ExitStack() as ctx:
        def sb(name, shape, dt=F32):
            return ctx.enter_context(nc.sbuf_tensor(name, shape, dt))

        def sem(name):
            return ctx.enter_context(nc.semaphore(name))

        raw = sb("raw", [P128, NRAW, CHUNK])
        w_hi = sb("w_hi", [P128, NW, CHUNK], F32R)
        w_lo = sb("w_lo", [P128, NW, CHUNK], F32R)
        act_hi = sb("act_hi", [P128, KT, TOK], F32R)
        act_lo = sb("act_lo", [P128, KT, TOK], F32R)
        xy = sb("xy", [P128, KT, TOK])
        vec = sb("vec", [P128, N_VEC])
        ident = sb("ident", [P128, P128])
        ones = sb("ones", [P128, P128])
        inv_d = sb("inv_d", [P128, 1])
        inv_hd = sb("inv_hd", [P128, P128])
        ln_shift = sb("ln_shift", [P128, 1])
        minus_half = sb("minus_half", [P128, TB])
        mod1 = sb("mod1", [P128, KT, 2])
        modr = sb("modr", [P128, 4, KT])
        amul = sb("amul", [P128, 2, KT])
        part1 = sb("part1", [P128, KT, 2, 2])
        sum1 = sb("sum1", [P128, 2, 2])
        partr = sb("partr", [P128, 8, 2])
        sumr = sb("sumr", [P128, 8])
        tok_v = sb("tok_v", [P128, TB])
        tok_r = sb("tok_r", [P128, TB])
        scratch = sb("scratch", [P128, 9, TOK])

        def pair(i):
            return scratch[:, i:i + 2, :]

        sq, hf, hm = pair(0), pair(2), pair(4)
        ssq, r_all, diag = scratch[:, 6], scratch[:, 7], scratch[:, 8]
        sq_head, ve = scratch[:, 0], scratch[:, 1]
        o_sb, d_sb = scratch[:, 2], scratch[:, 3]
        rot_a, rot_b = scratch[:, 4], scratch[:, 5]
        rs0, rs1, y_part = scratch[:, 6], scratch[:, 7], scratch[:, 8]

        heads = ExitStack()

        def sbh(name, shape, dt=F32):
            return heads.enter_context(nc.sbuf_tensor(name, shape, dt))

        ada_sb = sbh("ada_sb", [P128, NADA, HALF])
        silu_c = sbh("silu_c", [P128, D])
        rot_sb = sbh("rot_sb", [P128, 2, TOK])
        decay_sb = sbh("decay_sb", [P128, TOK])
        q_t = sbh("q_t", [P128, TOK])
        k_t = sbh("k_t", [P128, TOK])
        v_t = sbh("v_t", [P128, TOK])
        v_tok = sbh("v_tok", [P128, TB, P128])
        gate = sbh("gate", [P128, TOK])
        strips = sbh("strips", [P128, STRIPS])
        prob = sbh("prob", [P128, 2, STRIPS])
        mask_f = sbh("mask_f", [P128, P128])
        mask = sbh("mask", [P128, P128], BF16)
        ident_b = sbh("ident_b", [P128, P128], BF16)
        top = sbh("top", [P128, 8])
        ntop = sbh("ntop", [P128, 8])
        total = sbh("total", [P128, 8])
        rtotal = sbh("rtotal", [P128, 8])
        r_first = sbh("r_first", [P128, 4])
        lam_in = sbh("lam_in", [P128, 4, DQK])
        lam_prod = sbh("lam_prod", [P128, 2, DQK])
        lam_sum = sbh("lam_sum", [P128, 2])
        lam_exp = sbh("lam_exp", [P128, 2])
        neg_lam = sbh("neg_lam", [P128, 1])
        heads.close()
        u_hi = sb("u_hi", [P128, BLOCKS, TOK], F32R)
        u_lo = sb("u_lo", [P128, BLOCKS, TOK], F32R)
        relu = sb("relu", [P128, 2, TOK])
        usq = sb("usq", [P128, 2, TOK])

        bank = [ctx.enter_context(nc.psum_tensor(f"bank{i}", [P128, TOK], F32)) for i in range(8)]
        ps_a, ps_b, ps_c, ps_d = bank[4:8]

        c_landed, vec_landed = sem("c_landed"), sem("vec_landed")
        lam_landed, ident_landed, mask_landed = sem("lam_landed"), sem("ident_landed"), sem("mask_landed")
        rot_landed, decay_landed = sem("rot_landed"), sem("decay_landed")
        raw_landed = [sem(f"raw_landed{i}") for i in range(NRAW)]
        ada_landed = [sem(f"ada_landed{i}") for i in range(NADA)]
        x_landed = [sem(f"x_landed{i}") for i in range(KT // 2)]
        hi_ready, lo_ready, chunk_done = sem("hi_ready"), sem("lo_ready"), sem("chunk_done")
        const_ready, setup_ready = sem("const_ready"), sem("setup_ready")
        silu_ready, dot_done = sem("silu_ready"), sem("dot_done")
        mod_summed, mod_ready, scale_ready = sem("mod_summed"), sem("mod_ready"), sem("scale_ready")
        modr_summed, modr_ready = sem("modr_summed"), sem("modr_ready")
        lam_dotted, lam_exped, lam_ready = sem("lam_dotted"), sem("lam_exped"), sem("lam_ready")
        sq_ready, ssq_ready = sem("sq_ready"), sem("ssq_ready")
        mean_done, tok_v_ready, tok_r_ready = sem("mean_done"), sem("tok_v_ready"), sem("tok_r_ready")
        diag_ready, spread_done, r_all_ready = sem("diag_ready"), sem("spread_done"), sem("r_all_ready")
        hf_ready, hm_ready = sem("hf_ready"), sem("hm_ready")
        act_hi_ready, act_ready = sem("act_hi_ready"), sem("act_ready")
        q_read, k_read, q_ready, k_ready = sem("q_read"), sem("k_read"), sem("q_ready"), sem("k_ready")
        v_ready, gate_ready, gate_free = sem("v_ready"), sem("gate_ready"), sem("gate_free")
        scores_done, scores2_done, strips_ready = sem("scores_done"), sem("scores2_done"), sem("strips_ready")
        v_turned, v_tok_ready = sem("v_turned"), sem("v_tok_ready")
        o_done, o_ready, centre_done, d_ready = sem("o_done"), sem("o_ready"), sem("centre_done"), sem("d_ready")
        sq_head_ready, var_done, ve_ready = sem("sq_head_ready"), sem("var_done"), sem("ve_ready")
        ln_ready, rs0_ready, rs_ready = sem("ln_ready"), sem("rs0_ready"), sem("rs_ready")
        newton, half_ready, turned = sem("newton"), sem("half_ready"), sem("turned")
        y_part_ready, y_dif_ready, root_gated = sem("y_part_ready"), sem("y_dif_ready"), sem("root_gated")
        top_ready, ntop_ready, prob_ready = sem("top_ready"), sem("ntop_ready"), sem("prob_ready")
        top2_ready, ntop2_ready, prob2_ready = sem("top2_ready"), sem("ntop2_ready"), sem("prob2_ready")
        rtotal_ready, r_first_ready = sem("rtotal_ready"), sem("r_first_ready")
        second_ready, diff_ready, diff_turned = sem("second_ready"), sem("diff_ready"), sem("diff_turned")
        bank_free = [sem(f"bank_free{i}") for i in range(4)]
        relu_ready, u_hi_ready, usq_ready, u_ready = sem("relu_ready"), sem("u_hi_ready"), sem("usq_ready"), sem("u_ready")
        z_ready, z_turned, tile_ready = sem("z_ready"), sem("z_turned"), sem("tile_ready")
        scaled_v, scaled_s = sem("scaled_v"), sem("scaled_s")
        out_written = sem("out_written")

        block = ctx.enter_context(nc.Block())

        @block.sync
        def _(sp):
            def load_raw(s):
                r = s.place(NRAW)
                if s.above(NRAW):
                    sp.wait_ge(lo_ready, s.value(1, 1 - NRAW))
                sp.dma_start(raw[:, r], weights[s.value()]).then_inc(raw_landed[r], 16)

            def load_ada(a):
                r = a.place(NADA)
                if a.above(NADA):
                    sp.wait_ge(dot_done, a.value(1, 1 - NADA))
                sp.dma_start(ada_sb[:, r], ada[a.value()]).then_inc(ada_landed[r], 16)

            sp.dma_start(silu_c[:], c.partition_broadcast(P128)).then_inc(c_landed, 16)
            for a in range(NADA):
                load_ada(Count(a))
            for p in range(KT // 2):
                sp.dma_start(xy[:, 2 * p:2 * p + 2], x_t[:, 2 * p:2 * p + 2]).then_inc(x_landed[p], 16)
            load_raw(Count(0))
            for p in range(8):
                for a in range(8 * p + 4, min(8 * p + 12, A_RET)):
                    load_ada(Count(a))
                if p < 7:
                    load_raw(Count(p + 1))
            with sp.Fori(1, NRET) as h:
                for j in range(8):
                    load_raw(Count(j, (8, h)))
                    for e in range(2):
                        load_ada(Count(A_RET - 16 + 2 * j + e, (16, h)))
                sp.wait_ge(strips_ready, h)
                sp.dma_start(decay_sb[:], decay[h]).then_inc(decay_landed, 16)
            a = A_RET + 16 * (NRET - 1)
            for j in range(6):
                load_raw(Count(C_DIF + j))
                for _ in range(4 if j < 2 else 2):
                    load_ada(Count(a))
                    a += 1
                if j == 1:
                    sp.wait_ge(k_ready, NRET)
                    sp.dma_start(rot_sb[:, 0], rot[1, 0]).then_inc(rot_landed, 16)
                    sp.dma_start(rot_sb[:, 1], rot[1, 1]).then_inc(rot_landed, 16)
            for s in range(C_DIF + 6, C_DIF + 12):
                load_raw(Count(s))
            with sp.Fori(0, 9) as i:
                for j in range(4):
                    load_raw(Count(C_DIF + 12 + j, (4, i)))
            for s in range(C_OUT, C_OUT + 12):
                if s >= C_OUT + 4:
                    p = s - C_OUT - 4
                    sp.wait_ge(act_ready, KT + 2 * p + 2)
                    sp.dma_start(xy[:, 2 * p:2 * p + 2], x_t[:, 2 * p:2 * p + 2]).then_inc(x_landed[p], 16)
                load_raw(Count(s))
            with sp.Fori(0, (N_CHUNKS - C_OUT - 12) // 4) as i:
                for j in range(4):
                    load_raw(Count(C_OUT + 12 + j, (4, i)))
            for tb in range(TB):
                if tb < 3:
                    sp.wait_ge(scaled_v, tb + 1)
                else:
                    sp.wait_ge(scaled_s, 1)
                sp.dma_start(out[tb * P128:(tb + 1) * P128, :].rearrange("p (k f) -> p k f", f=P128),
                             xy[:, :, tb * P128:(tb + 1) * P128]).then_inc(out_written, 16)
            sp.wait_ge(out_written, 16 * TB)

        @block.tensor
        def _(pe):
            def split_products(pairs, s):
                w = s.place(NW)
                pe.wait_ge(hi_ready, s.value(1, 1))
                for i, acc, hi, lo, first, _, ready in pairs:
                    if ready is not None:
                        pe.wait_ge(*ready)
                    stationary = w_hi[:, w, i * P128:(i + 1) * P128]
                    pe.matmul(acc[:], stationary, hi, start=first, stop=False)
                    pe.matmul(acc[:], stationary, lo, start=False, stop=False)
                pe.wait_ge(lo_ready, s.value(1, 1))
                for i, acc, hi, _, _, last, _ in pairs:
                    mm = pe.matmul(acc[:], w_lo[:, w, i * P128:(i + 1) * P128], hi, start=False, stop=last)
                mm.then_inc(chunk_done, 1)

            def tile_chunk(s, b, half):
                split_products([(i, bank[b], act_hi[:, 8 * half + i], act_lo[:, 8 * half + i],
                                 half == 0 and i == 0, half == 1 and i == BLOCKS - 1, None)
                                for i in range(BLOCKS)], s)

            def quad_chunk(s, j, ready0):
                split_products([(i, bank[i % 4], act_hi[:, 2 * j + i // 4], act_lo[:, 2 * j + i // 4],
                                 j == 0 and i < 4, j == 7 and i >= 4,
                                 (act_ready, ready0 + 2 * j + i // 4 + 1) if i % 4 == 0 else None)
                                for i in range(BLOCKS)], s)

            def token_scale(n):
                pe.wait_ge(ssq_ready, [KT, 2 * KT, 3 * KT][n - 1])
                for tb in range(TB):
                    mm = pe.matmul(ps_a[:, tb:tb + 1], ssq[:, tb * P128:(tb + 1) * P128], inv_d[:], start=True, stop=True)
                mm.then_inc(mean_done, 1)
                if n < 3:
                    pe.wait_ge(diag_ready, n)
                    pe.matmul(ps_b[:], ones[:], diag, start=True, stop=True).then_inc(spread_done, 1)

            def ret_scores(hp):
                pe.wait_ge(q_ready, hp + 1)
                pe.wait_ge(k_ready, hp + 1)
                for jb, (acc, at) in enumerate([(ps_a, 0), (ps_b, 0), (ps_c, 0), (ps_c, 256)]):
                    n = TOK - jb * P128
                    mm = pe.matmul(acc[:, at:at + n], k_t[:, jb * P128:(jb + 1) * P128], q_t[:, jb * P128:],
                                   start=True, stop=True)
                mm.then_inc(scores_done, 1)

            def dif_scores(hp, blocks, done):
                for ib, (first, second), at in blocks:
                    n = (ib + 1) * P128
                    for comp, acc in enumerate((first, second)):
                        rows = slice(comp * DQK, (comp + 1) * DQK)
                        pe.matmul(acc[:, at:at + n], q_t[rows, ib * P128:(ib + 1) * P128], k_t[rows, 0:n],
                                  start=True, stop=False)
                        mm = pe.matmul(acc[:, at + n - P128:at + n], ident_b[:], mask[:], start=False, stop=True)
                mm.then_inc(done, 1)

            def dif_scores1(hp):
                pe.wait_ge(q_ready, hp + 1)
                pe.wait_ge(k_ready, hp + 1)
                pe.wait_ge(ve_ready, hp)
                dif_scores(hp, [(3, (ps_a, ps_b), 0), (2, (ps_c, ps_d), 0)], scores_done)

            def dif_scores2(hp):
                pe.wait_ge(prob_ready, hp - NRET + 1)
                dif_scores(hp, [(1, (ps_a, ps_b), 0), (0, (ps_a, ps_b), 256)], scores2_done)

            def turn_v(hp):
                pe.wait_ge(v_ready, hp + 1)
                for tb in range(TB):
                    mm = pe.transpose(ps_d[:, tb * P128:(tb + 1) * P128], v_t[:, tb * P128:(tb + 1) * P128], ident[:])
                mm.then_inc(v_turned, 1)

            def turn_diff(hp):
                pe.wait_ge(diff_ready, hp - NRET + 1)
                for jb, (acc, at) in enumerate([(ps_a, 0), (ps_b, 0), (ps_c, 0), (ps_c, 256)]):
                    for ib in range(jb, TB):
                        to = at + (ib - jb) * P128
                        mm = pe.transpose(acc[:, to:to + P128],
                                          prob[:, 0, ROWS[ib] + jb * P128:ROWS[ib] + (jb + 1) * P128], ident[:])
                mm.then_inc(diff_turned, 1)

            def head_out(hp):
                pe.wait_ge(strips_ready, hp + 1)
                pe.wait_ge(v_tok_ready, hp + 1)
                for jb in range(TB):
                    mm = pe.matmul(ps_a[:, jb * P128:], v_tok[:, jb], strips[:, STRIP[jb]:STRIP[jb] + TOK - jb * P128],
                                   start=(jb == 0), stop=(jb == TB - 1), skip_group_check=True)
                mm.then_inc(o_done, 1)

            def ret_centre(hp):
                pe.wait_ge(o_ready, hp + 1)
                pe.matmul(ps_b[:], inv_hd[:], o_sb, start=True, stop=True).then_inc(centre_done, 1)

            def head_var(hp):
                pe.wait_ge(sq_head_ready, hp + 1)
                pe.matmul(ps_c[:], inv_hd[:], sq_head, start=True, stop=True).then_inc(var_done, 1)

            ret_stage = {0: ret_scores, 1: turn_v, 2: head_out, 3: ret_centre, 4: head_var}
            dif_stage = {0: dif_scores1, 1: dif_scores2, 2: turn_v, 3: turn_diff, 4: head_out, 5: head_var}

            def project_ret(h, s0):
                for j in range(8):
                    if j in ret_stage:
                        ret_stage[j](h - 1)
                    if j % 2 == 0:
                        pe.wait_ge((q_read, k_read, v_ready, gate_ready)[j // 2], h)
                    tile_chunk(s0 + j, j // 2, j % 2)

            def project_dif(h, s0, stage):
                for j in range(6):
                    if j in stage:
                        stage[j](h - 1)
                    if j % 2 == 0:
                        pe.wait_ge((q_read, k_read, v_ready)[j // 2], h)
                    tile_chunk(s0 + j, j // 2, j % 2)

            pe.wait_ge(setup_ready, 1)
            pe.wait_ge(const_ready, 4)
            token_scale(1)
            for j in range(8):
                quad_chunk(Count(j), j, 0)
            with pe.Fori(1, NRET) as h:
                project_ret(h, Count(0, (8, h)))
            project_dif(NRET, Count(C_DIF), ret_stage)
            project_dif(NRET + 1, Count(C_DIF + 6), dif_stage)
            with pe.Fori(0, 3) as i:
                for e in range(2):
                    project_dif(2 * i + (NRET + 2 + e), Count(C_DIF + 12 + 6 * e, (12, i)), dif_stage)
            for j in range(8):
                if j in dif_stage:
                    dif_stage[j](NRET + NDIF - 1)
                if j == 0:
                    for s, n in ((q_read, 16), (k_read, 16), (v_ready, 16), (gate_ready, NRET)):
                        pe.wait_ge(s, n)
                quad_chunk(Count(C_OUT + j), j, KT)
            with pe.Fori(1, 4) as g:
                for t in range(4):
                    pe.wait_ge(bank_free[t], g)
                    for half in range(2):
                        tile_chunk(Count(C_OUT + 2 * t + half, (8, g)), t, half)
            token_scale(2)

            def up_tile(g, t, q, s):
                pe.wait_ge(bank_free[t], 4 * g + 4)
                pe.wait_ge(relu_ready, 8 * g + 4 * q + t - 3)
                for half in range(2):
                    tile_chunk(s + half, t, half)

            def down_tile(g, t, q, s, first_wait):
                pe.wait_ge(bank_free[t], 4 * g + 4 + q)
                split_products([(i, bank[t], u_hi[:, i], u_lo[:, i], i == 0, i == BLOCKS - 1,
                                 (u_ready, 8 * g + i + 1) if first_wait else None) for i in range(BLOCKS)], s)

            def up_group(g, s0):
                with pe.Fori(0, 2) as q:
                    for t in range(4):
                        up_tile(g, t, q, Count(s0.base + 2 * t, *s0.terms, (8, q)))

            def down_group(g, s0):
                with pe.Fori(0, 4) as q:
                    for t in range(4):
                        down_tile(g, t, q, Count(s0.base + t, *s0.terms, (4, q)), t == 0)

            for t in range(4):
                pe.wait_ge(bank_free[t], 4)
            for j in range(8):
                quad_chunk(Count(C_MLP + j), j, 2 * KT)
            for t in range(4):
                up_tile(0, t, 1, Count(C_MLP + 8 + 2 * t))
            down_group(0, Count(C_MLP + 16))
            with pe.Fori(1, MLP_GROUPS - 1) as g:
                up_group(g, Count(C_MLP, (PER_GROUP, g)))
                down_group(g, Count(C_MLP + 16, (PER_GROUP, g)))
            g = MLP_GROUPS - 1
            s0 = Count(C_MLP + PER_GROUP * g)
            up_group(g, s0)

            def turn_tile(m):
                pe.wait_ge(z_ready, m + 1)
                if m >= 2:
                    pe.wait_ge(tile_ready, m - 1)
                for tb in range(TB):
                    mm = pe.transpose(bank[4 + m % 2][:, tb * P128:(tb + 1) * P128],
                                      hf[:, m % 2, tb * P128:(tb + 1) * P128], ident[:])
                mm.then_inc(z_turned, 1)

            for m in range(KT):
                down_tile(g, m % 4, m // 4, s0 + (16 + m), m == 0)
                if m >= 1:
                    turn_tile(m - 1)
            turn_tile(KT - 1)
            pe.wait_ge(tile_ready, KT - 1)
            token_scale(3)

        @block.scalar
        def _(act):
            def round_w(s):
                r, w = s.place(NRAW), s.place(NW)
                act.wait_ge(raw_landed[r], 16 * s.value(NRAW, 1))
                if s.above(NW):
                    act.wait_ge(chunk_done, s.value(1, 1 - NW))
                nc.scalar.activation(w_hi[:, w], raw[:, r], ACT.Copy).then_inc(hi_ready, 1)

            def spread(n):
                act.wait_ge(spread_done, n)
                nc.scalar.activation(r_all, ps_b[:], ACT.Copy).then_inc(r_all_ready, 1)

            def modulated_hi(n, k, n_scale):
                act.wait_ge(scale_ready, n_scale)
                act.wait_ge(hf_ready, KT * n + k + 1)
                shift = mod1[:, k, 1:2] if n == 0 else modr[:, 1, k:k + 1]
                nc.scalar.activation(act_hi[:, k], hf[:, k % 2], ACT.Identity, bias=shift,
                                     scale=amul[:, n, k:k + 1]).then_inc(act_hi_ready, 1)

            def square_x(m, x_wait):
                act.wait_ge(*x_wait)
                if m % KT >= 2:
                    act.wait_ge(ssq_ready, m - 1)
                nc.scalar.activation(sq[:, m % 2], xy[:, m % KT], ACT.Square).then_inc(sq_ready, 1)

            def take_gate(hp):
                act.wait_ge(chunk_done, 8 * hp + 8)
                act.wait_ge(gate_free, hp + 1)
                nc.scalar.activation(gate[:], bank[3][:], ACT.Silu).then_inc(gate_ready, 1)

            def take_v(h, s_end):
                act.wait_ge(chunk_done, s_end.value())
                nc.scalar.activation(v_t[:], bank[2][:], ACT.Copy).then_inc(v_ready, 1)

            def take_v_tok(hp):
                act.wait_ge(v_turned, hp + 1)
                nc.scalar.activation(v_tok[:].rearrange("p a b -> p (a b)"), ps_d[:], ACT.Copy).then_inc(v_tok_ready, 1)

            def take_o(hp):
                act.wait_ge(o_done, hp + 1)
                nc.scalar.activation(o_sb, ps_a[:], ACT.Copy).then_inc(o_ready, 1)

            def square_d(hp):
                act.wait_ge(d_ready, hp + 1)
                nc.scalar.activation(sq_head, d_sb, ACT.Square).then_inc(sq_head_ready, 1)

            def square_o(hp):
                act.wait_ge(o_ready, hp + 1)
                nc.scalar.activation(sq_head, o_sb, ACT.Square).then_inc(sq_head_ready, 1)

            def second_term(hp):
                act.wait_ge(r_first_ready, hp - NRET + 1)
                for ib in range(TB):
                    cols = slice(ROWS[ib], ROWS[ib] + (ib + 1) * P128)
                    op = nc.scalar.activation(prob[:, 1, cols], prob[:, 1, cols], ACT.Copy, scale=r_first[:, ib:ib + 1])
                op.then_inc(second_ready, 1)
                take_v_tok(hp)

            def rough_root(hp):
                act.wait_ge(half_ready, 2)
                act.wait_ge(ve_ready, hp + 1)
                nc.scalar.activation(rs0, ve, ACT.Ln, scale=LN_SCALE).then_inc(ln_ready, 1)
                act.wait_ge(ln_ready, hp + 1)
                nc.scalar.activation(rs0, rs0, ACT.Exp, scale=-0.5, bias=ln_shift[:, 0:1]).then_inc(rs0_ready, 1)

            def softmax(hp, blocks, ready, done):
                act.wait_ge(ready, hp - NRET + 1)
                for ib, banks, at in blocks:
                    n = (ib + 1) * P128
                    for comp, acc in enumerate(banks):
                        u = 4 * comp + ib
                        e = nc.scalar.activation(prob[:, comp, ROWS[ib]:ROWS[ib] + n], acc[:, at:at + n], ACT.Exp,
                                                 bias=ntop[:, u:u + 1], scale=QK_SCALE, accum_out=total[:, u:u + 1])
                e.then_inc(done, 1)

            def softmax1(hp):
                softmax(hp, [(3, (ps_a, ps_b), 0), (2, (ps_c, ps_d), 0)], ntop_ready, prob_ready)

            def softmax2(hp):
                softmax(hp, [(1, (ps_a, ps_b), 0), (0, (ps_a, ps_b), 256)], ntop2_ready, prob2_ready)

            ret_stage = {0: take_gate, 1: take_v_tok, 2: take_o, 3: square_d, 4: rough_root}
            dif_stage = {0: softmax1, 1: softmax2, 2: second_term, 4: square_o, 5: rough_root}

            def head_ret(h, s0):
                for j in range(8):
                    round_w(s0 + (j + 1))
                    if j in ret_stage:
                        ret_stage[j](h - 1)
                    if j == 6:
                        take_v(h, s0 + 6)

            def head_dif(h, s0, stage):
                for j in range(6):
                    round_w(s0 + (j + 1))
                    if j == 0 and stage is dif_stage:
                        take_v(h - 1, s0)
                    if j in stage:
                        stage[j](h - 1)

            act.dma_start(vec[:], vecs).then_inc(vec_landed, 16)
            act.dma_start(ident[:], ident_in).then_inc(ident_landed, 16)
            act.dma_start(lam_in[:], lams.partition_broadcast(P128)).then_inc(lam_landed, 16)
            act.dma_start(mask_f[:], mask_in).then_inc(mask_landed, 16)
            act.wait_ge(c_landed, 16)
            nc.scalar.activation(silu_c[:], silu_c[:], ACT.Silu).then_inc(silu_ready, 1)
            act.dma_start(rot_sb[:, 0], rot[0, 0]).then_inc(rot_landed, 16)
            act.dma_start(rot_sb[:, 1], rot[0, 1]).then_inc(rot_landed, 16)
            act.dma_start(decay_sb[:], decay[0]).then_inc(decay_landed, 16)
            for m in range(KT):
                square_x(m, (x_landed[m // 2], 16))
            round_w(Count(0))
            spread(1)
            modulated_hi(0, 0, 1)
            modulated_hi(0, 1, 1)
            for j in range(8):
                if j < 7:
                    modulated_hi(0, 2 * j + 2, j + 2)
                    modulated_hi(0, 2 * j + 3, j + 2)
                round_w(Count(j + 1))
                if j == 7:
                    act.wait_ge(lam_dotted, 1)
                    nc.scalar.activation(lam_exp[:], lam_sum[:], ACT.Exp).then_inc(lam_exped, 1)
            take_v(0, Count(8))
            with act.Fori(1, NRET) as h:
                head_ret(h, Count(0, (8, h)))
            head_dif(NRET, Count(C_DIF), ret_stage)
            head_dif(NRET + 1, Count(C_DIF + 6), dif_stage)
            with act.Fori(0, 3) as i:
                for e in range(2):
                    head_dif(2 * i + (NRET + 2 + e), Count(C_DIF + 12 + 6 * e, (12, i)), dif_stage)

            def split_y(k):
                if k < NRET:
                    act.wait_ge(gate_free, k + 2)
                else:
                    act.wait_ge(y_dif_ready, k - NRET + 1)
                nc.scalar.activation(act_hi[:, k], xy[:, k], ACT.Copy).then_inc(act_hi_ready, 1)

            take_v(NRET + NDIF - 1, Count(C_OUT))
            split_y(0)
            split_y(1)
            for j in range(8):
                round_w(Count(C_OUT + j + 1))
                if j < 7:
                    split_y(2 * j + 2)
                    split_y(2 * j + 3)
                if j in dif_stage:
                    dif_stage[j](NRET + NDIF - 1)
            for m in range(4):
                square_x(KT + m, (bank_free[m % 4], m // 4 + 1))
            for g in range(1, 4):
                for t in range(4):
                    for half in range(2):
                        round_w(Count(C_OUT + 8 * g + 2 * t + half + 1))
                    m = 4 * g + t
                    square_x(KT + m, (bank_free[m % 4], m // 4 + 1))
            spread(2)
            modulated_hi(1, 0, 9)
            modulated_hi(1, 1, 9)
            for j in range(8):
                if j < 7:
                    modulated_hi(1, 2 * j + 2, 9)
                    modulated_hi(1, 2 * j + 3, 9)
                round_w(Count(C_MLP + j + 1))

            def take_u(g, i, t, s_end):
                n = 8 * g + i
                act.wait_ge(chunk_done, s_end.value())
                if not isinstance(n, int) or n >= 2:
                    act.wait_ge(u_ready, n - 1)
                nc.scalar.activation(relu[:, t % 2], bank[t][:], ACT.Relu).then_inc(relu_ready, 1)
                act.wait_ge(relu_ready, n + 1)
                nc.scalar.activation(u_hi[:, i], relu[:, t % 2], ACT.Square).then_inc(u_hi_ready, 1)

            def up_quad(g, q, s0):
                for t in range(4):
                    for half in range(2):
                        round_w(s0 + (2 * t + half + 1))
                    take_u(g, 4 * q + t, t, s0 + (2 * t + 2))

            def down_group(s0):
                with act.Fori(0, 4) as q:
                    for t in range(4):
                        round_w(Count(s0.base + t + 1, *s0.terms, (4, q)))

            for t in range(4):
                take_u(0, t, t, Count(C_MLP + 8))
            up_quad(0, 1, Count(C_MLP + 8))
            down_group(Count(C_MLP + 16))
            with act.Fori(1, MLP_GROUPS - 1) as g:
                with act.Fori(0, 2) as q:
                    up_quad(g, q, Count(C_MLP, (PER_GROUP, g), (8, q)))
                down_group(Count(C_MLP + 16, (PER_GROUP, g)))
            g = MLP_GROUPS - 1
            s0 = C_MLP + PER_GROUP * g
            with act.Fori(0, 2) as q:
                up_quad(g, q, Count(s0, (8, q)))
            for m in range(KT):
                if m < KT - 1:
                    round_w(Count(s0 + 17 + m))
                square_x(2 * KT + m, (bank_free[m % 4], 4 + 4 * g + m // 4 + 1))
                if m >= 2:
                    act.wait_ge(z_turned, m - 1)
                nc.scalar.activation(hf[:, m % 2], xy[:, m], ACT.Copy,
                                     scale=vec[:, V_FIN + m:V_FIN + m + 1]).then_inc(z_ready, 1)
            act.wait_ge(tok_r_ready, 3)
            act.wait_ge(tile_ready, KT)
            last = xy[:, :, 3 * P128:]
            nc.scalar.activation(last, last, ACT.Copy, scale=tok_r[:, 3:4]).then_inc(scaled_s, 1)

        @block.vector
        def _(dve):
            def rest_w(s):
                r, w = s.place(NRAW), s.place(NW)
                dve.wait_ge(hi_ready, s.value(1, 1))
                nc.vector.tensor_tensor(w_lo[:, w], raw[:, r], w_hi[:, w].bitcast(F32), ALU.subtract).then_inc(lo_ready, 1)

            def dot_ada(a, to):
                r = a.place(NADA)
                dve.wait_ge(ada_landed[r], 16 * a.value(NADA, 1))
                half = r % 2
                nc.vector.tensor_tensor_reduce(ada_sb[:, r], ada_sb[:, r], silu_c[:, half * HALF:(half + 1) * HALF],
                                               1.0, 0.0, ALU.mult, ALU.add, to).then_inc(dot_done, 1)

            def modulation1(p):
                for k in range(2 * p, 2 * p + 2):
                    for e in range(4):
                        dot_ada(Count(4 * k + e), part1[:, k, e // 2, e % 2:e % 2 + 1])
                ks = slice(2 * p, 2 * p + 2)
                dve.wait_ge(dot_done, 8 * p + 8)
                nc.vector.tensor_tensor(sum1[:], part1[:, ks, :, 0], part1[:, ks, :, 1], ALU.add).then_inc(mod_summed, 1)
                dve.wait_ge(mod_summed, p + 1)
                bias = vec[:, V_B1 + 4 * p:V_B1 + 4 * p + 4].rearrange("p (a b) -> p a b", b=2)
                nc.vector.tensor_tensor(mod1[:, ks], sum1[:], bias, ALU.add).then_inc(mod_ready, 1)
                dve.wait_ge(mod_ready, p + 1)
                nc.vector.scalar_tensor_tensor(amul[:, 0, ks], mod1[:, ks, 0], 1.0,
                                               vec[:, V_N1 + 2 * p:V_N1 + 2 * p + 2], ALU.add, ALU.mult)\
                    .then_inc(scale_ready, 1)

            def token_scale(n):
                dve.wait_ge(mean_done, n)
                nc.vector.tensor_scalar(tok_v[:], ps_a[:, 0:TB], NORM_EPS, None, ALU.add).then_inc(tok_v_ready, 1)
                dve.wait_ge(tok_r_ready, n)
                if n < 3:
                    nc.vector.tensor_tensor(diag.rearrange("p (a b) -> p a b", a=TB),
                                            ident[:].unsqueeze(1).broadcast_to([P128, TB, P128]),
                                            tok_r[:].unsqueeze(2).broadcast_to([P128, TB, P128]), ALU.mult)\
                        .then_inc(diag_ready, 1)

            def modulated_rest(n, k):
                dve.wait_ge(scale_ready, k // 2 + 1 if n == 0 else KT // 2 + 1)
                dve.wait_ge(hf_ready, KT * n + k + 1)
                shift = mod1[:, k, 1:2] if n == 0 else modr[:, 1, k:k + 1]
                nc.vector.tensor_scalar(hm[:, k % 2], hf[:, k % 2], amul[:, n, k:k + 1], shift, ALU.mult, ALU.add)\
                    .then_inc(hm_ready, 1)
                dve.wait_ge(hm_ready, KT * n + k + 1)
                dve.wait_ge(act_hi_ready, 2 * KT * n + k + 1)
                nc.vector.tensor_tensor(act_lo[:, k], hm[:, k % 2], act_hi[:, k].bitcast(F32), ALU.subtract)\
                    .then_inc(act_ready, 1)

            def sum_square(m):
                dve.wait_ge(sq_ready, m + 1)
                if m % KT:
                    dve.wait_ge(ssq_ready, m)
                    nc.vector.tensor_tensor(ssq, ssq, sq[:, m % 2], ALU.add).then_inc(ssq_ready, 1)
                else:
                    nc.vector.tensor_copy(ssq, sq[:, m % 2]).then_inc(ssq_ready, 1)

            def rotate(h, src, s_end, read, ready, to, dif):
                n = 2 * h + (1 if ready is k_ready else 0)
                dve.wait_ge(chunk_done, s_end.value())
                if ready is k_ready:
                    dve.wait_ge(q_ready, h + 1)
                dve.wait_ge(rot_landed, 64 if dif else 32)
                cos, sin = rot_sb[:, 0], rot_sb[:, 1]
                nc.vector.tensor_tensor(rot_a, src[:], cos, ALU.mult)
                if dif:
                    nc.vector.stream_shuffle(rot_b, src[:], [(i + 8) % 16 if i < 16 else i for i in range(32)])\
                        .then_inc(read, 1)
                    dve.wait_ge(read, h + 1)
                    nc.vector.tensor_tensor(rot_b, rot_b, sin, ALU.mult).then_inc(turned, 1)
                    dve.wait_ge(turned, n - 2 * NRET + 1)
                else:
                    nc.vector.tensor_tensor(rot_b[0:64], src[64:128], sin[64:128], ALU.mult)
                    nc.vector.tensor_tensor(rot_b[64:128], src[0:64], sin[0:64], ALU.mult).then_inc(read, 1)
                    dve.wait_ge(read, h + 1)
                nc.vector.tensor_tensor(to[:], rot_a, rot_b, ALU.add).then_inc(ready, 1)

            def rotate_q(h, s_end, dif):
                rotate(h, bank[0], s_end, q_read, q_ready, q_t, dif)

            def rotate_k(h, s_end, dif):
                rotate(h, bank[1], s_end, k_read, k_ready, k_t, dif)

            def decay_strips(hp):
                dve.wait_ge(scores_done, hp + 1)
                dve.wait_ge(decay_landed, 16 * hp + 16)
                for jb, (acc, at) in enumerate([(ps_a, 0), (ps_b, 0), (ps_c, 0), (ps_c, 256)]):
                    n = TOK - jb * P128
                    op = nc.vector.tensor_tensor(strips[:, STRIP[jb]:STRIP[jb] + n], acc[:, at:at + n],
                                                 decay_sb[:, 0:n], ALU.mult)
                op.then_inc(strips_ready, 1)

            def centre(hp):
                dve.wait_ge(centre_done, hp + 1)
                nc.vector.tensor_tensor(d_sb, o_sb, ps_b[:], ALU.subtract).then_inc(d_ready, 1)

            def var_eps(hp):
                dve.wait_ge(var_done, hp + 1)
                nc.vector.tensor_scalar(ve, ps_c[:], GN_EPS, BIG, ALU.add, ALU.min).then_inc(ve_ready, 1)

            def finish_ret(hp):
                dve.wait_ge(rs_ready, hp + 1)
                dve.wait_ge(gate_ready, hp + 1)
                weight = vec[:, V_HEAD + hp:V_HEAD + hp + 1] if isinstance(hp, int) else vec[:, bass.ds(hp + V_HEAD, 1)]
                nc.vector.scalar_tensor_tensor(y_part, d_sb, weight, rs1, ALU.mult, ALU.mult).then_inc(y_part_ready, 1)
                dve.wait_ge(y_part_ready, hp + 1)
                to = xy[:, hp] if isinstance(hp, int) else xy[:, bass.ds(hp, 1)].squeeze(1)
                nc.vector.tensor_tensor(to, y_part, gate[:], ALU.mult).then_inc(gate_free, 1)

            def clamp_o(hp):
                dve.wait_ge(o_done, hp + 1)
                nc.vector.tensor_scalar(o_sb, ps_a[:], SQUARE_TOP, -SQUARE_TOP, ALU.min, ALU.max).then_inc(o_ready, 1)

            def finish_dif(hp):
                dve.wait_ge(rs_ready, hp + 1)
                nc.vector.scalar_tensor_tensor(rs1, ve, MEAN_TOP, rs1, ALU.is_lt, ALU.mult).then_inc(root_gated, 1)
                dve.wait_ge(root_gated, hp - NRET + 1)
                weight = vec[:, V_HEAD + hp:V_HEAD + hp + 1] if isinstance(hp, int) else vec[:, bass.ds(hp + V_HEAD, 1)]
                to = xy[:, hp] if isinstance(hp, int) else xy[:, bass.ds(hp, 1)].squeeze(1)
                nc.vector.scalar_tensor_tensor(to, o_sb, weight, rs1, ALU.mult, ALU.mult).then_inc(y_dif_ready, 1)

            def row_tops(hp, blocks, scores, found, ready):
                dve.wait_ge(scores, hp + 1 if scores is scores_done else hp - NRET + 1)
                for ib, banks, at in blocks:
                    n = (ib + 1) * P128
                    for comp, acc in enumerate(banks):
                        op = nc.vector.reduce_max(top[:, 4 * comp + ib:4 * comp + ib + 1], acc[:, at:at + n], AX_X)
                op.then_inc(found, 1)
                dve.wait_ge(found, hp - NRET + 1)
                first = blocks[-1][0]
                cols = [t[:].rearrange("p (a b) -> p a b", a=2)[:, :, first:first + 2] for t in (ntop, top)]
                nc.vector.tensor_scalar(cols[0], cols[1], -QK_SCALE, None, ALU.mult).then_inc(ready, 1)

            def tops1(hp):
                row_tops(hp, [(3, (ps_a, ps_b), 0), (2, (ps_c, ps_d), 0)], scores_done, top_ready, ntop_ready)

            def tops2(hp):
                row_tops(hp, [(1, (ps_a, ps_b), 0), (0, (ps_a, ps_b), 256)], scores2_done, top2_ready, ntop2_ready)

            def combine(hp):
                n = hp - NRET + 1
                dve.wait_ge(prob2_ready, n)
                nc.vector.reciprocal(rtotal[:], total[:]).then_inc(rtotal_ready, 1)
                dve.wait_ge(rtotal_ready, n)
                dve.wait_ge(lam_ready, 1)
                nc.vector.tensor_scalar(r_first[:], rtotal[:, 4:8], neg_lam[:, 0:1], None, ALU.mult).then_inc(r_first_ready, 1)
                dve.wait_ge(second_ready, n)
                for ib in range(TB):
                    cols = slice(ROWS[ib], ROWS[ib] + (ib + 1) * P128)
                    op = nc.vector.scalar_tensor_tensor(prob[:, 0, cols], prob[:, 0, cols], rtotal[:, ib:ib + 1],
                                                        prob[:, 1, cols], ALU.mult, ALU.add)
                op.then_inc(diff_ready, 1)

            def diff_strips(hp):
                dve.wait_ge(diff_turned, hp - NRET + 1)
                for acc, at, n in ((ps_a, STRIP[0], 512), (ps_b, STRIP[1], 384), (ps_c, STRIP[2], 384)):
                    op = nc.vector.tensor_copy(strips[:, at:at + n], acc[:, 0:n])
                op.then_inc(strips_ready, 1)

            def modulation_rest(a, part):
                for e in range(2):
                    dot_ada(a + e, partr[:, part, e:e + 1])

            def modulation_sum(n, col):
                dve.wait_ge(dot_done, 16 * n + A_RET)
                nc.vector.tensor_tensor(sumr[:], partr[:, :, 0], partr[:, :, 1], ALU.add).then_inc(modr_summed, 1)
                dve.wait_ge(modr_summed, n)
                flat = modr[:].rearrange("p a b -> p (a b)")
                to = flat[:, bass.ds(col, 8)] if not isinstance(col, int) else flat[:, col:col + 8]
                bias = vec[:, bass.ds(col + V_B, 8)] if not isinstance(col, int) else vec[:, V_B + col:V_B + col + 8]
                nc.vector.tensor_tensor(to, sumr[:], bias, ALU.add).then_inc(modr_ready, 1)

            def head_ret(h, s0):
                for j in range(8):
                    rest_w(s0 + (j + 1))
                    if j == 0:
                        decay_strips(h - 1)
                    if j == 2:
                        rotate_q(h, s0 + 2, False)
                    if j == 3:
                        centre(h - 1)
                    if j == 4:
                        var_eps(h - 1)
                        rotate_k(h, s0 + 4, False)
                    if j == 7:
                        finish_ret(h - 1)
                    modulation_rest(Count(A_RET - 16 + 2 * j, (16, h)), j)
                modulation_sum(h, 8 * h - 8)

            def head_dif(h, s0):
                for j in range(6):
                    rest_w(s0 + (j + 1))
                    if j == 0:
                        tops1(h - 1)
                    if j == 1:
                        tops2(h - 1)
                        if not isinstance(h, int) or h > NRET + 1:
                            finish_dif(h - 2)
                    if j == 2:
                        combine(h - 1)
                        rotate_q(h, s0 + 2, True)
                    if j == 3:
                        diff_strips(h - 1)
                    if j == 4:
                        clamp_o(h - 1)
                        rotate_k(h, s0 + 4, True)
                    if j == 5:
                        var_eps(h - 1)

            nc.vector.memset(ones[:], 1.0).then_inc(const_ready, 1)
            nc.vector.memset(inv_d[:], 1.0 / D).then_inc(const_ready, 1)
            nc.vector.memset(inv_hd[:], 1.0 / HD).then_inc(const_ready, 1)
            nc.vector.memset(part1[:], 0.0).then_inc(gate_free, 1)
            dve.wait_ge(gate_free, 1)
            dve.wait_ge(ident_landed, 16)
            dve.wait_ge(mask_landed, 16)
            nc.vector.tensor_copy(ident_b[:], ident[:]).then_inc(const_ready, 1)
            nc.vector.tensor_copy(mask[:], mask_f[:]).then_inc(setup_ready, 1)
            dve.wait_ge(vec_landed, 16)
            dve.wait_ge(silu_ready, 1)
            modulation1(0)
            for m in range(KT):
                sum_square(m)
            rest_w(Count(0))
            token_scale(1)
            modulated_rest(0, 0)
            modulated_rest(0, 1)
            for j in range(8):
                if j < 7:
                    modulation1(j + 1)
                    modulated_rest(0, 2 * j + 2)
                    modulated_rest(0, 2 * j + 3)
                if j == 6:
                    dve.wait_ge(lam_landed, 16)
                    for e in range(2):
                        op = nc.vector.tensor_tensor_reduce(lam_prod[:, e], lam_in[:, 2 * e], lam_in[:, 2 * e + 1], 1.0, 0.0,
                                                            ALU.mult, ALU.add, lam_sum[:, e:e + 1])
                    op.then_inc(lam_dotted, 1)
                    dif_w = vec[:, V_HEAD + NRET:V_HEAD + NRET + NDIF]
                    nc.vector.tensor_scalar(dif_w, dif_w, 1.0 - LAM_INIT, None, ALU.mult).then_inc(setup_ready, 1)
                rest_w(Count(j + 1))
            dve.wait_ge(lam_exped, 1)
            nc.vector.tensor_scalar(neg_lam[:], lam_exp[:, 1:2], lam_exp[:, 0:1], LAM_INIT, ALU.subtract, ALU.subtract)\
                .then_inc(lam_ready, 1)
            rotate_q(0, Count(8), False)
            rotate_k(0, Count(8), False)
            with dve.Fori(1, NRET) as h:
                head_ret(h, Count(0, (8, h)))
            a = A_RET + 16 * (NRET - 1)
            part = 0
            for j in range(6):
                rest_w(Count(C_DIF + j + 1))
                if j == 0:
                    decay_strips(NRET - 1)
                if j == 2:
                    rotate_q(NRET, Count(C_DIF + 2), True)
                if j == 3:
                    centre(NRET - 1)
                if j == 4:
                    var_eps(NRET - 1)
                    rotate_k(NRET, Count(C_DIF + 4), True)
                if j == 5:
                    finish_ret(NRET - 1)
                for _ in range(2 if j < 2 else 1):
                    modulation_rest(Count(a), part)
                    a, part = a + 2, part + 1
            modulation_sum(NRET, 8 * NRET - 8)
            dve.wait_ge(modr_ready, NRET)
            nc.vector.scalar_tensor_tensor(amul[:, 1], modr[:, 2], 1.0, vec[:, V_N2:V_N2 + KT], ALU.add, ALU.mult)\
                .then_inc(scale_ready, 1)
            head_dif(NRET + 1, Count(C_DIF + 6))
            with dve.Fori(0, 3) as i:
                for e in range(2):
                    head_dif(2 * i + (NRET + 2 + e), Count(C_DIF + 12 + 6 * e, (12, i)))

            def split_y(k):
                dve.wait_ge(act_hi_ready, KT + k + 1)
                nc.vector.tensor_tensor(act_lo[:, k], xy[:, k], act_hi[:, k].bitcast(F32), ALU.subtract).then_inc(act_ready, 1)

            split_y(0)
            split_y(1)
            hp = NRET + NDIF - 1
            for j in range(8):
                rest_w(Count(C_OUT + j + 1))
                if j == 0:
                    tops1(hp)
                if j == 1:
                    tops2(hp)
                    finish_dif(hp - 1)
                if j == 2:
                    combine(hp)
                if j == 3:
                    diff_strips(hp)
                if j == 4:
                    clamp_o(hp)
                if j == 5:
                    var_eps(hp)
                if j == 6:
                    finish_dif(hp)
                if j < 7:
                    split_y(2 * j + 2)
                    split_y(2 * j + 3)

            def residual(part, m, t, s_end):
                dve.wait_ge(chunk_done, s_end.value())
                if isinstance(m, int):
                    to, gate_col = xy[:, m], modr[:, part, m:m + 1]
                else:
                    to, gate_col = xy[:, bass.ds(m, 1)].squeeze(1), modr[:, part, bass.ds(m, 1)]
                nc.vector.scalar_tensor_tensor(to, bank[t][:], gate_col, to, ALU.mult, ALU.add).then_inc(bank_free[t], 1)

            def residual_out(m, s_end):
                dve.wait_ge(x_landed[m // 2], 32)
                residual(0, m, m % 4, s_end)

            for m in range(4):
                residual_out(m, Count(C_OUT + 8))
                sum_square(KT + m)
            for g in range(1, 4):
                for t in range(4):
                    for half in range(2):
                        rest_w(Count(C_OUT + 8 * g + 2 * t + half + 1))
                    m = 4 * g + t
                    residual_out(m, Count(C_OUT + 2 * m + 2))
                    sum_square(KT + m)
            token_scale(2)
            modulated_rest(1, 0)
            modulated_rest(1, 1)
            for j in range(8):
                if j < 7:
                    modulated_rest(1, 2 * j + 2)
                    modulated_rest(1, 2 * j + 3)
                rest_w(Count(C_MLP + j + 1))

            def rest_u(g, i, t):
                n = 8 * g + i
                dve.wait_ge(relu_ready, n + 1)
                nc.vector.tensor_tensor(usq[:, t % 2], relu[:, t % 2], relu[:, t % 2], ALU.mult).then_inc(usq_ready, 1)
                dve.wait_ge(usq_ready, n + 1)
                dve.wait_ge(u_hi_ready, n + 1)
                nc.vector.tensor_tensor(u_lo[:, i], usq[:, t % 2], u_hi[:, i].bitcast(F32), ALU.subtract).then_inc(u_ready, 1)

            def up_quad(g, q, s0):
                for t in range(4):
                    for half in range(2):
                        rest_w(s0 + (2 * t + half + 1))
                    rest_u(g, 4 * q + t, t)

            def down_group(s0):
                with dve.Fori(0, 4) as q:
                    for t in range(4):
                        done = Count(s0.base + t + 1, *s0.terms, (4, q))
                        rest_w(done)
                        residual(3, 4 * q + t, t, done)

            for t in range(4):
                rest_u(0, t, t)
            up_quad(0, 1, Count(C_MLP + 8))
            down_group(Count(C_MLP + 16))
            with dve.Fori(1, MLP_GROUPS - 1) as g:
                with dve.Fori(0, 2) as q:
                    up_quad(g, q, Count(C_MLP, (PER_GROUP, g), (8, q)))
                down_group(Count(C_MLP + 16, (PER_GROUP, g)))
            g = MLP_GROUPS - 1
            s0 = C_MLP + PER_GROUP * g
            with dve.Fori(0, 2) as q:
                up_quad(g, q, Count(s0, (8, q)))

            def take_tile(m):
                dve.wait_ge(z_turned, m + 1)
                nc.vector.tensor_copy(xy[:, m], bank[4 + m % 2][:]).then_inc(tile_ready, 1)

            for m in range(KT):
                if m < KT - 1:
                    rest_w(Count(s0 + 17 + m))
                residual(3, m, m % 4, Count(s0 + 17 + m))
                if m >= 1:
                    take_tile(m - 1)
                sum_square(2 * KT + m)
            take_tile(KT - 1)
            token_scale(3)
            dve.wait_ge(tile_ready, KT)
            for tb in range(3):
                tile = xy[:, :, tb * P128:(tb + 1) * P128]
                nc.vector.tensor_scalar(tile, tile, tok_r[:, tb:tb + 1], None, ALU.mult).then_inc(scaled_v, 1)

        @block.gpsimd
        def _(pool):
            def normed(n, k):
                pool.wait_ge(r_all_ready, n + 1)
                if KT * n + k >= 2:
                    pool.wait_ge(hm_ready, KT * n + k - 1)
                    if k >= 2:
                        pool.wait_ge(act_hi_ready, 2 * KT * n + k - 1)
                nc.gpsimd.tensor_tensor(hf[:, k % 2], xy[:, k], r_all, ALU.mult).then_inc(hf_ready, 1)

            def token_root(n):
                pool.wait_ge(tok_v_ready, n)
                nc.gpsimd.tensor_tensor(tok_r[:], tok_v[:], minus_half[:], ALU.pow).then_inc(tok_r_ready, 1)

            def refine_root(hp):
                pool.wait_ge(rs0_ready, hp + 1)
                nc.gpsimd.tensor_tensor(rs1, ve, rs0, ALU.mult).then_inc(newton, 1)
                pool.wait_ge(newton, 3 * hp + 1)
                nc.gpsimd.tensor_tensor(rs1, rs1, rs0, ALU.mult).then_inc(newton, 1)
                pool.wait_ge(newton, 3 * hp + 2)
                nc.gpsimd.tensor_scalar(rs1, rs1, -0.5, 1.5, ALU.mult, ALU.add).then_inc(newton, 1)
                pool.wait_ge(newton, 3 * hp + 3)
                nc.gpsimd.tensor_tensor(rs1, rs1, rs0, ALU.mult).then_inc(rs_ready, 1)

            nc.gpsimd.memset(ln_shift[:], 0.5 * float(np.log(LN_SCALE))).then_inc(half_ready, 1)
            nc.gpsimd.memset(minus_half[:], -0.5).then_inc(half_ready, 1)
            pool.wait_ge(half_ready, 2)
            token_root(1)
            for k in range(KT):
                normed(0, k)
            for hp in range(NRET + NDIF):
                refine_root(hp)
            token_root(2)
            for k in range(KT):
                normed(1, k)
            token_root(3)


def blocks_of(w):
    k, m = w.shape
    return w.reshape(k // P128, P128, m // P128, P128).transpose(0, 2, 1, 3)


def tile_chunks(blocks, ms):
    n_k = blocks.shape[0]
    b = blocks[:, ms].reshape(n_k // BLOCKS, BLOCKS, len(ms), P128, P128)
    return b.transpose(2, 0, 3, 1, 4).reshape(-1, P128, CHUNK)


def quad_chunks(blocks, ms):
    b = blocks[:, ms].reshape(8, 2, 4, P128, P128)
    return b.transpose(0, 3, 1, 2, 4).reshape(-1, P128, CHUNK)


def weight_chunks(w_in, w_out, w1, w2):
    b_in, b_out, b_up, b_down = (blocks_of(w) for w in (w_in, w_out, w1, w2))
    order = [[h, NRET + h, 2 * NRET + h, 3 * NRET + h] for h in range(NRET)]
    order += [[4 * NRET + d, 4 * NRET + NDIF + d, 4 * NRET + 2 * NDIF + d] for d in range(NDIF)]
    parts = [quad_chunks(b_in, order[0])] + [tile_chunks(b_in, ms) for ms in order[1:]]
    parts += [quad_chunks(b_out, [0, 1, 2, 3]), tile_chunks(b_out, list(range(4, KT)))]
    for g in range(MLP_GROUPS):
        ms = list(range(BLOCKS * g, BLOCKS * g + BLOCKS))
        parts += [quad_chunks(b_up, ms[:4]), tile_chunks(b_up, ms[4:])] if g == 0 else [tile_chunks(b_up, ms)]
        parts.append(tile_chunks(b_down[ms], list(range(KT))))
    return np.concatenate(parts)


def ada_rows(w_ada):
    cols = w_ada.T.reshape(6, KT, P128, 2, HALF).transpose(0, 1, 3, 2, 4)
    first = np.stack([cols[1], cols[0]], axis=1).reshape(-1, P128, HALF)
    rest = np.stack([cols[2], cols[3], cols[4], cols[5]]).reshape(-1, P128, HALF)
    return np.concatenate([first, rest])


def columns(v):
    return v.reshape(-1, P128).T


def packed_vectors(b_ada, norm1_w, norm2_w, final_norm_w, ret_gn_w, diff_subln_w):
    b = b_ada.reshape(6, KT, P128)
    b1 = np.stack([b[1], b[0]], axis=1).reshape(-1)
    rest = np.concatenate([b[2], b[3], b[4], b[5]]).reshape(-1)
    return np.concatenate([columns(v) for v in (b1, rest, norm1_w, norm2_w, final_norm_w, ret_gn_w, diff_subln_w)],
                          axis=1)


def rotary_tables():
    f = np.float32
    pos = np.arange(TOK, dtype=f)
    out = np.zeros((2, 2, P128, TOK), f)
    inv = f(10000.0) ** (-np.arange(0, HD, 2, dtype=f) / f(HD))
    ang = inv[:, None] * pos[None, :]
    out[0, 0] = np.tile(np.cos(ang), (2, 1))
    out[0, 1] = np.concatenate([np.sin(ang), -np.sin(ang)])
    rot_dim = DQK // 4
    inv = f(500000.0) ** (-np.arange(0, rot_dim, 2, dtype=f) / f(rot_dim))
    ang = inv[:, None] * pos[None, :]
    out[1, 0] = 1.0
    for at in (0, DQK):
        out[1, 0, at:at + rot_dim] = np.tile(np.cos(ang), (2, 1))
        out[1, 1, at:at + rot_dim] = np.concatenate([-np.sin(ang), np.sin(ang)])
    return out


def decay_tables():
    lg = np.log(np.float32(1.0) - np.float32(2.0) ** (np.float32(-5.0) - np.arange(NRET, dtype=np.float32)))
    rel = np.arange(TOK)[None, :] - np.arange(P128)[:, None]
    d = np.exp(np.maximum(rel, 0)[None] * lg.astype(np.float64)[:, None, None]) * float(HD) ** -0.5
    return np.where(rel[None] >= 0, d, 0.0).astype(np.float32)


def kernel(x, c, w_ada, b_ada, norm1_w, norm2_w, w_in, ret_gn_w, diff_lq1, diff_lk1, diff_lq2, diff_lk2,
           diff_subln_w, w_out, w_mlp1, w_mlp2, final_norm_w):
    import concourse.bacc as bacc
    from concourse.bass_utils import run_bass_kernel_spmd

    rows = np.arange(P128)
    arrays = {
        "x_t": x[0].T.reshape(KT, P128, TOK).transpose(1, 0, 2),
        "c_row": c[0],
        "ada": ada_rows(w_ada[0]),
        "weights": weight_chunks(w_in[0], w_out[0], w_mlp1[0], w_mlp2[0]),
        "vecs": packed_vectors(b_ada[0], norm1_w[0], norm2_w[0], final_norm_w, ret_gn_w[0], diff_subln_w[0]),
        "lams": np.stack([diff_lq1[0], diff_lk1[0], diff_lq2[0], diff_lk2[0]]),
        "rot": rotary_tables(),
        "decay": decay_tables(),
        "ident_in": np.eye(P128, dtype=np.float32),
        "mask_in": np.where(rows[None, :] <= rows[:, None], 0.0, -1e30).astype(np.float32),
    }
    arrays = {name: np.ascontiguousarray(a) for name, a in arrays.items()}
    nc = bacc.Bacc("TRN2", target_bir_lowering=False, num_devices=1)
    aps = [nc.dram_tensor(name, a.shape, mybir.dt.from_np(a.dtype), kind="ExternalInput").ap()
           for name, a in arrays.items()]
    out = nc.dram_tensor("out", (TOK, D), F32, kind="ExternalOutput").ap()
    block_kernel(nc, *aps, out)
    r = run_bass_kernel_spmd(nc, [arrays], core_ids=[0])
    return r.results[0]["out"].reshape(1, TOK, D)
```

```python
from contextlib import ExitStack

import numpy as np

import concourse.bass as bass
from concourse import mybir

F32 = mybir.dt.float32
F32R = mybir.dt.float32r
BF16 = mybir.dt.bfloat16
ALU = mybir.AluOpType
ACT = mybir.ActivationFunctionType
AX_X = mybir.AxisListType.X

P128 = 128
D = 2048
TOK = 512
KT = D // P128
TB = TOK // P128
HD = 128
NRET = 8
NDIF = 8
DQK = HD // 2
FF = 4 * D
HALF = D // 2
NORM_EPS = 1e-6
GN_EPS = 1e-5
LAM_INIT = 0.8 - 0.6
QK_SCALE = float(DQK) ** -0.5
SQUARE_TOP = 1.8446e19
MEAN_TOP = 2.658e36

LN_SCALE = 2.0 ** -64

BLOCKS = 8
CHUNK = BLOCKS * P128
NRAW = 4
NW = 2
NADA = 4
NADA_1 = 6
MLP_GROUPS = FF // P128 // BLOCKS

EARLY = 4
FIRST = KT
C_DIF = FIRST + 6 * EARLY + 8 * (NRET - 1 - EARLY)
C_OUT = C_DIF + 6 * NDIF
C_MLP = C_OUT + 2 * KT
PER_GROUP = 4 * BLOCKS
N_CHUNKS = C_MLP + PER_GROUP * MLP_GROUPS
A_RET = 4 * KT
N_ADA = 12 * KT

ADA_6 = (1, 1, 1, 2, 1, 2)
ADA_8 = (1,) * 8
Y_SPLITS = ((2, 3, 4), (5, 6, 7), (8, 9), (10, 11, 12), (13, 14), (), (15,))

STRIP = [0, 512, 896, 1152]
STRIPS = 1280
ROWS = [0, 128, 384, 768]

V_B1, V_B, V_N1, V_N2, V_FIN, V_HEAD = 0, 32, 96, 112, 128, 144
N_VEC = 160


class Count:

    def __init__(self, base, *terms):
        self.base, self.terms = base, terms

    def __add__(self, n):
        return Count(self.base + n, *self.terms)

    def value(self, per=1, add=0):
        total = self.base // per + add
        for factor, register in self.terms:
            assert factor % per == 0
            total = (factor // per) * register + total
        return total

    def place(self, ring):
        assert all(factor % ring == 0 for factor, _ in self.terms)
        return self.base % ring

    def above(self, n):
        return bool(self.terms) or self.base >= n


def ada_place(a):
    if not a.above(A_RET):
        return a.base % NADA_1, a.base // NADA_1 + 1
    return a.place(NADA), a.value(NADA, 1 + -(-A_RET // NADA_1) - A_RET // NADA)


def block_kernel(nc, x_t, c, ada, weights, vecs, lams, rot, decay, ident_in, mask_in, out):
    with ExitStack() as ctx:
        def sb(name, shape, dt=F32):
            return ctx.enter_context(nc.sbuf_tensor(name, shape, dt))

        def sem(name):
            return ctx.enter_context(nc.semaphore(name))

        raw = sb("raw", [P128, NRAW, CHUNK])
        w_hi = sb("w_hi", [P128, NW, CHUNK], F32R)
        w_lo = sb("w_lo", [P128, NW, CHUNK], F32R)
        act_hi = sb("act_hi", [P128, KT, TOK], F32R)
        act_lo = sb("act_lo", [P128, KT, TOK], F32R)
        xy = sb("xy", [P128, KT, TOK])
        vec = sb("vec", [P128, N_VEC])
        ident = sb("ident", [P128, P128])
        ones = sb("ones", [P128, P128])
        inv_d = sb("inv_d", [P128, 1])
        inv_hd = sb("inv_hd", [P128, P128], F32R)
        ident_r = sb("ident_r", [P128, P128], F32R)
        ln_shift = sb("ln_shift", [P128, 1])
        minus_half = sb("minus_half", [P128, TB])
        mod1 = sb("mod1", [P128, KT, 2])
        modr = sb("modr", [P128, 4, KT])
        amul = sb("amul", [P128, 2, KT])
        part1 = sb("part1", [P128, KT, 2, 2])
        sum1 = sb("sum1", [P128, 2, 2])
        partr = sb("partr", [P128, 8, 2])
        sumr = sb("sumr", [P128, 8])
        tok_v = sb("tok_v", [P128, TB])
        tok_r = sb("tok_r", [P128, TB])

        def in_turn(*groups):
            made = []
            for i, group in enumerate(groups):
                stack = ctx if i == len(groups) - 1 else ExitStack()
                made += [stack.enter_context(nc.sbuf_tensor(name, shape, dt)) for name, shape, dt in group]
                if stack is not ctx:
                    stack.close()
            return made

        pair, row = [P128, 2, TOK], [P128, TOK]
        sq, sq_head, ve = in_turn([("sq", pair, F32)], [("sq_head", row, F32), ("ve", row, F32)])
        hf, o_sb, sq_hi = in_turn([("hf", pair, F32)], [("o_sb", row, F32), ("sq_hi", row, F32R)])
        hm, _, v_lo, rot_a, rot_b = in_turn([("hm", pair, F32)], [("rot_0", row, F32), ("v_lo", row, F32R)],
                                            [("rot_a", row, F32), ("rot_b", row, F32)])
        ssq, rs0 = in_turn([("ssq", row, F32)], [("rs0", row, F32)])
        r_all, rs1 = in_turn([("r_all", row, F32)], [("rs1", row, F32)])
        diag, sq_lo = in_turn([("diag", row, F32)], [("sq_lo", row, F32R)])
        ssq, rs0, r_all, rs1, diag = ssq[:], rs0[:], r_all[:], rs1[:], diag[:]
        sq_head, ve, o_sb, sq_hi, sq_lo = sq_head[:], ve[:], o_sb[:], sq_hi[:], sq_lo[:]
        rot_a, rot_b = rot_a[:], rot_b[:]

        heads = ExitStack()

        def sbh(name, shape, dt=F32):
            return heads.enter_context(nc.sbuf_tensor(name, shape, dt))

        ada_sb = sbh("ada_sb", [P128, NADA, HALF])
        silu_c = sbh("silu_c", [P128, D])
        rot_sb = sbh("rot_sb", [P128, 2, TOK])
        decay_sb = sbh("decay_sb", [P128, TOK])
        q_hi = sbh("q_hi", [P128, TOK], F32R)
        q_lo = sbh("q_lo", [P128, TOK], F32R)
        k_hi = sbh("k_hi", [P128, TOK], F32R)
        k_lo = sbh("k_lo", [P128, TOK], F32R)
        v_hi = sbh("v_hi", [P128, TOK], F32R)
        v_tok = sbh("v_tok", [P128, TB, P128])
        v_sum = sbh("v_sum", [P128, TB])
        v_mean = sbh("v_mean", [P128, TB])
        strips = sbh("strips", [P128, STRIPS])
        prob = sbh("prob", [P128, 2, STRIPS])


        def ada_at(r):
            if r < NADA:
                return ada_sb[:, r]
            return prob[:].rearrange("p a b -> p (a b)")[:, (r - NADA) * HALF:(r - NADA + 1) * HALF]

        early = prob[:].rearrange("p a b -> p (a b)")[:, (NADA_1 - NADA) * HALF:]
        lam_in = early[:, 0:4 * DQK].rearrange("p (a b) -> p a b", a=4)
        lam_prod = early[:, 4 * DQK:6 * DQK].rearrange("p (a b) -> p a b", a=2)
        mask_f = early[:, 6 * DQK:6 * DQK + P128]

        mask = sbh("mask", [P128, P128], BF16)
        ident_b = sbh("ident_b", [P128, P128], BF16)
        top = sbh("top", [P128, 8])
        ntop = sbh("ntop", [P128, 8])
        total = sbh("total", [P128, 8])
        rtotal = sbh("rtotal", [P128, 8])
        r_first = sbh("r_first", [P128, 4])
        lam_sum = sbh("lam_sum", [P128, 2])
        lam_exp = sbh("lam_exp", [P128, 2])
        neg_lam = sbh("neg_lam", [P128, 1])
        heads.close()
        u_hi = sb("u_hi", [P128, BLOCKS, TOK], F32R)
        u_lo = sb("u_lo", [P128, BLOCKS, TOK], F32R)
        relu = sb("relu", [P128, 2, TOK])
        usq = sb("usq", [P128, 2, TOK])

        bank = [ctx.enter_context(nc.psum_tensor(f"bank{i}", [P128, TOK], F32)) for i in range(8)]
        ps_a, ps_b, ps_c, ps_d = bank[4:8]

        c_landed, vec_landed = sem("c_landed"), sem("vec_landed")
        lam_landed, ident_landed, mask_landed = sem("lam_landed"), sem("ident_landed"), sem("mask_landed")
        rot_landed, decay_landed = sem("rot_landed"), sem("decay_landed")
        raw_landed = [sem(f"raw_landed{i}") for i in range(NRAW)]
        ada_landed = [sem(f"ada_landed{i}") for i in range(NADA_1)]
        x_landed = [sem(f"x_landed{i}") for i in range(KT // 2)]
        hi_ready, lo_ready, chunk_done = sem("hi_ready"), sem("lo_ready"), sem("chunk_done")
        const_ready, setup_ready = sem("const_ready"), sem("setup_ready")
        silu_ready, dot_done = sem("silu_ready"), sem("dot_done")
        mod_summed, mod_ready, scale_ready = sem("mod_summed"), sem("mod_ready"), sem("scale_ready")
        modr_summed, modr_ready = sem("modr_summed"), sem("modr_ready")
        lam_dotted, lam_exped, lam_ready = sem("lam_dotted"), sem("lam_exped"), sem("lam_ready")
        sq_ready, ssq_ready = sem("sq_ready"), sem("ssq_ready")
        mean_done, tok_v_ready, tok_r_ready = sem("mean_done"), sem("tok_v_ready"), sem("tok_r_ready")
        diag_ready, spread_done, r_all_ready = sem("diag_ready"), sem("spread_done"), sem("r_all_ready")
        hf_ready, hm_ready = sem("hf_ready"), sem("hm_ready")
        act_hi_ready, act_ready = sem("act_hi_ready"), sem("act_ready")
        q_read, k_read, q_ready, k_ready = sem("q_read"), sem("k_read"), sem("q_ready"), sem("k_ready")
        v_ready, gate_ready, y_ret_ready = sem("v_ready"), sem("gate_ready"), sem("y_ret_ready")
        v_summed, v_mean_ready = sem("v_summed"), sem("v_mean_ready")
        scores_done, scores2_done, strips_ready = sem("scores_done"), sem("scores2_done"), sem("strips_ready")
        v_turned, v_tok_ready = sem("v_turned"), sem("v_tok_ready")
        o_done, o_ready = sem("o_done"), sem("o_ready")
        sq_head_ready, var_done, ve_ready = sem("sq_head_ready"), sem("var_done"), sem("ve_ready")
        ln_ready, rs0_ready, rs_ready = sem("ln_ready"), sem("rs0_ready"), sem("rs_ready")
        newton, half_ready, turned = sem("newton"), sem("half_ready"), sem("turned")
        rotated_hi, rotated = sem("rotated_hi"), sem("rotated")
        wide_read = sem("wide_read")
        v_hi_ready, sq_lo_ready = sem("v_hi_ready"), sem("sq_lo_ready")
        y_part_ready, y_dif_ready, root_gated = sem("y_part_ready"), sem("y_dif_ready"), sem("root_gated")
        top_ready, ntop_ready, prob_ready = sem("top_ready"), sem("ntop_ready"), sem("prob_ready")
        top2_ready, ntop2_ready, prob2_ready = sem("top2_ready"), sem("ntop2_ready"), sem("prob2_ready")
        rtotal_ready, r_first_ready = sem("rtotal_ready"), sem("r_first_ready")
        second_ready, diff_ready, diff_turned = sem("second_ready"), sem("diff_ready"), sem("diff_turned")
        bank_free = [sem(f"bank_free{i}") for i in range(4)]
        relu_ready, u_hi_ready, usq_ready, u_ready = sem("relu_ready"), sem("u_hi_ready"), sem("usq_ready"), sem("u_ready")
        z_ready, z_turned, tile_ready = sem("z_ready"), sem("z_turned"), sem("tile_ready")
        scaled_v, scaled_s = sem("scaled_v"), sem("scaled_s")
        out_written = sem("out_written")

        block = ctx.enter_context(nc.Block())

        @block.sync
        def _(sp):
            def load_raw(s):
                r = s.place(NRAW)
                if s.above(NRAW):
                    sp.wait_ge(lo_ready, s.value(1, 1 - NRAW))
                sp.dma_start(raw[:, r], weights[s.value()]).then_inc(raw_landed[r], 16)

            def load_ada(a):
                r = ada_place(a)[0]
                ring = NADA if a.above(A_RET) else NADA_1
                if a.above(ring):
                    sp.wait_ge(dot_done, a.value(1, 1 - ring))
                sp.dma_start(ada_at(r), ada[a.value()]).then_inc(ada_landed[r], 16)

            def load_phase(h, s0, slots):
                part = 0
                for j in range(len(slots)):
                    load_raw(s0 + (j + 2))
                    for _ in range(2 * slots[j]):
                        load_ada(Count(A_RET - 16 + part, (16, h)) if not isinstance(h, int)
                                 else Count(A_RET - 16 + 16 * h + part))
                        part += 1
                    if j == 2 and (not isinstance(h, int) or h < NRET):
                        sp.wait_ge(strips_ready, h)
                        sp.dma_start(decay_sb[:], decay[h]).then_inc(decay_landed, 16)

            sp.dma_start(silu_c[:], c.partition_broadcast(P128)).then_inc(c_landed, 16)
            for p in range(KT // 2):
                sp.dma_start(xy[:, 2 * p:2 * p + 2], x_t[:, 2 * p:2 * p + 2]).then_inc(x_landed[p], 16)
            for p in range(KT // 2):
                for a in range(8 * p, 8 * p + 8):
                    load_ada(Count(a))
                    if a % 8 in (2, 5):
                        load_raw(Count(2 * p + (a % 8) // 4))
            load_raw(Count(FIRST))
            load_raw(Count(FIRST + 1))
            for h in range(1, EARLY + 1):
                load_phase(h, Count(FIRST + 6 * (h - 1)), ADA_6)
            with sp.Fori(EARLY + 1, NRET) as h:
                load_phase(h, Count(C_DIF - 8 * NRET, (8, h)), ADA_8)
            sp.wait_ge(k_ready, NRET)
            sp.dma_start(rot_sb[:, 0], rot[1, 0]).then_inc(rot_landed, 16)
            sp.dma_start(rot_sb[:, 1], rot[1, 1]).then_inc(rot_landed, 16)
            load_phase(NRET, Count(C_DIF), ADA_6)
            with sp.Fori(0, 10) as i:
                for j in range(4):
                    load_raw(Count(C_DIF + 8 + j, (4, i)))
            for s in range(C_OUT, C_OUT + 12):
                if s >= C_OUT + 4:
                    p = s - C_OUT - 4
                    sp.wait_ge(act_ready, KT + 2 * p + 2)
                    sp.dma_start(xy[:, 2 * p:2 * p + 2], x_t[:, 2 * p:2 * p + 2]).then_inc(x_landed[p], 16)
                load_raw(Count(s))
            with sp.Fori(0, (N_CHUNKS - C_OUT - 12) // 4) as i:
                for j in range(4):
                    load_raw(Count(C_OUT + 12 + j, (4, i)))
            for tb in range(TB):
                if tb < 3:
                    sp.wait_ge(scaled_v, tb + 1)
                else:
                    sp.wait_ge(scaled_s, 1)
                sp.dma_start(out[tb * P128:(tb + 1) * P128, :].rearrange("p (k f) -> p k f", f=P128),
                             xy[:, :, tb * P128:(tb + 1) * P128]).then_inc(out_written, 16)
            sp.wait_ge(out_written, 16 * TB)

        @block.tensor
        def _(pe):
            def split_products(pairs, s):
                w = s.place(NW)
                pe.wait_ge(hi_ready, s.value(1, 1))
                for i, acc, hi, lo, first, _, ready in pairs:
                    if ready is not None:
                        pe.wait_ge(*ready)
                    stationary = w_hi[:, w, i * P128:(i + 1) * P128]
                    pe.matmul(acc[:], stationary, hi, start=first, stop=False)
                    pe.matmul(acc[:], stationary, lo, start=False, stop=False)
                pe.wait_ge(lo_ready, s.value(1, 1))
                for i, acc, hi, _, _, last, _ in pairs:
                    mm = pe.matmul(acc[:], w_lo[:, w, i * P128:(i + 1) * P128], hi, start=False, stop=last)
                mm.then_inc(chunk_done, 1)

            def tile_chunk(s, b, half):
                split_products([(i, bank[b], act_hi[:, 8 * half + i], act_lo[:, 8 * half + i],
                                 half == 0 and i == 0, half == 1 and i == BLOCKS - 1, None)
                                for i in range(BLOCKS)], s)

            def first_chunk(k):
                split_products([(i, bank[i], act_hi[:, k], act_lo[:, k], k == 0, k == KT - 1,
                                 (act_ready, k + 1) if i == 0 else None) for i in range(BLOCKS)], Count(k))

            def quad_chunk(s, j, ready0):
                split_products([(i, bank[i % 4], act_hi[:, 2 * j + i // 4], act_lo[:, 2 * j + i // 4],
                                 j == 0 and i < 4, j == 7 and i >= 4,
                                 (act_ready, ready0 + 2 * j + i // 4 + 1) if i % 4 == 0 else None)
                                for i in range(BLOCKS)], s)

            def token_scale(n):
                pe.wait_ge(ssq_ready, [KT, 2 * KT, 3 * KT][n - 1])
                for tb in range(TB):
                    mm = pe.matmul(ps_a[:, tb:tb + 1], ssq[:, tb * P128:(tb + 1) * P128], inv_d[:], start=True, stop=True)
                mm.then_inc(mean_done, 1)
                if n < 3:
                    pe.wait_ge(diag_ready, n)
                    pe.matmul(ps_b[:], ones[:], diag, start=True, stop=True).then_inc(spread_done, 1)

            def exact_product(acc, stationary, moving, start=True, stop=True):
                pe.matmul(acc, stationary[0], moving[0], start=start, stop=False)
                pe.matmul(acc, stationary[0], moving[1], start=False, stop=False)
                return pe.matmul(acc, stationary[1], moving[0], start=False, stop=stop)

            def exact_turn(acc, hi, lo):
                pe.matmul(acc, hi, ident_r[:], start=True, stop=False)
                return pe.matmul(acc, lo, ident_r[:], start=False, stop=True)

            def ret_scores(hp):
                pe.wait_ge(q_ready, hp + 1)
                pe.wait_ge(k_ready, hp + 1)
                for jb, (acc, at) in enumerate([(ps_a, 0), (ps_b, 0), (ps_c, 0), (ps_c, 256)]):
                    n = TOK - jb * P128
                    keys = slice(jb * P128, (jb + 1) * P128)
                    mm = exact_product(acc[:, at:at + n], (k_hi[:, keys], k_lo[:, keys]),
                                       (q_hi[:, jb * P128:], q_lo[:, jb * P128:]))
                mm.then_inc(scores_done, 1)

            def dif_scores(hp, blocks, done):
                for ib, (first, second), at in blocks:
                    n = (ib + 1) * P128
                    for comp, acc in enumerate((first, second)):
                        rows = slice(comp * DQK, (comp + 1) * DQK)
                        queries = slice(ib * P128, (ib + 1) * P128)
                        exact_product(acc[:, at:at + n], (q_hi[rows, queries], q_lo[rows, queries]),
                                      (k_hi[rows, 0:n], k_lo[rows, 0:n]), stop=False)
                        mm = pe.matmul(acc[:, at + n - P128:at + n], ident_b[:], mask[:], start=False, stop=True)
                mm.then_inc(done, 1)

            def dif_scores1(hp):
                pe.wait_ge(q_ready, hp + 1)
                pe.wait_ge(k_ready, hp + 1)
                pe.wait_ge(ve_ready, hp)
                dif_scores(hp, [(3, (ps_a, ps_b), 0), (2, (ps_c, ps_d), 0)], scores_done)

            def dif_scores2(hp):
                pe.wait_ge(wide_read, hp - NRET + 1)
                dif_scores(hp, [(1, (ps_a, ps_b), 0), (0, (ps_a, ps_b), 256)], scores2_done)

            def turn_v(hp):
                pe.wait_ge(v_ready, hp + 1)
                for tb in range(TB):
                    tokens = slice(tb * P128, (tb + 1) * P128)
                    mm = exact_turn(ps_d[:, tokens], v_hi[:, tokens], v_lo[:, tokens])
                mm.then_inc(v_turned, 1)

            def turn_diff(hp):
                pe.wait_ge(diff_ready, hp - NRET + 1)
                for jb, (acc, at) in enumerate([(ps_a, 0), (ps_b, 0), (ps_c, 0), (ps_c, 256)]):
                    for ib in range(jb, TB):
                        to = at + (ib - jb) * P128
                        mm = pe.transpose(acc[:, to:to + P128],
                                          prob[:, 0, ROWS[ib] + jb * P128:ROWS[ib] + (jb + 1) * P128], ident[:])
                mm.then_inc(diff_turned, 1)

            def head_out(hp):
                pe.wait_ge(strips_ready, hp + 1)
                pe.wait_ge(v_tok_ready, hp + 1)
                for jb in range(TB):
                    mm = pe.matmul(ps_a[:, jb * P128:], v_tok[:, jb], strips[:, STRIP[jb]:STRIP[jb] + TOK - jb * P128],
                                   start=(jb == 0), stop=(jb == TB - 1), skip_group_check=True)
                mm.then_inc(o_done, 1)

            def head_var(hp):
                pe.wait_ge(sq_lo_ready, hp + 1)
                pe.matmul(ps_c[:], inv_hd[:], sq_hi, start=True, stop=False)
                pe.matmul(ps_c[:], inv_hd[:], sq_lo, start=False, stop=True).then_inc(var_done, 1)

            def turn_dif_v(hp):
                pe.wait_ge(prob_ready, hp - NRET + 1)
                turn_v(hp)

            ret_stage = {0: ret_scores, 1: turn_v, 2: head_out, 4: head_var}
            dif_stage = {0: dif_scores1, 1: dif_scores2, 2: turn_dif_v, 3: turn_diff, 4: head_out, 5: head_var}

            def project(h, s0, slots, stage):
                for j in range(slots):
                    late = j == 0 and stage is ret_stage
                    if j in stage and not late:
                        stage[j](h - 1)
                    if j % 2 == 0:
                        pe.wait_ge((q_read, k_read, v_ready, gate_ready)[j // 2], h)
                    tile_chunk(s0 + j, j // 2, j % 2)
                    if late:
                        if isinstance(h, int) and h == 1:
                            pe.wait_ge(gate_ready, 1 + EARLY)
                        stage[j](h - 1)

            pe.wait_ge(setup_ready, 1)
            pe.wait_ge(const_ready, 4)
            token_scale(1)
            pe.wait_ge(r_all_ready, 1)
            for k in range(KT):
                first_chunk(k)
            for h in range(1, EARLY + 1):
                project(h, Count(FIRST + 6 * (h - 1)), 6, ret_stage)
            with pe.Fori(EARLY + 1, NRET) as h:
                project(h, Count(C_DIF - 8 * NRET, (8, h)), 8, ret_stage)
            project(NRET, Count(C_DIF), 6, ret_stage)
            project(NRET + 1, Count(C_DIF + 6), 6, dif_stage)
            with pe.Fori(0, 3) as i:
                for e in range(2):
                    project(2 * i + (NRET + 2 + e), Count(C_DIF + 12 + 6 * e, (12, i)), 6, dif_stage)
            for j in range(8):
                if j in dif_stage:
                    dif_stage[j](NRET + NDIF - 1)
                if j == 0:
                    for s, n in ((q_read, 16), (k_read, 16), (v_ready, 16), (gate_ready, NRET)):
                        pe.wait_ge(s, n)
                quad_chunk(Count(C_OUT + j), j, KT)
            with pe.Fori(1, 4) as g:
                for t in range(4):
                    pe.wait_ge(bank_free[t], g)
                    for half in range(2):
                        tile_chunk(Count(C_OUT + 2 * t + half, (8, g)), t, half)
            token_scale(2)

            def up_tile(g, t, q, s):
                pe.wait_ge(bank_free[t], 4 * g + 4)
                pe.wait_ge(relu_ready, 8 * g + 4 * q + t - 3)
                for half in range(2):
                    tile_chunk(s + half, t, half)

            def down_tile(g, t, q, s, first_wait):
                pe.wait_ge(bank_free[t], 4 * g + 4 + q)
                split_products([(i, bank[t], u_hi[:, i], u_lo[:, i], i == 0, i == BLOCKS - 1,
                                 (u_ready, 8 * g + i + 1) if first_wait else None) for i in range(BLOCKS)], s)

            def up_group(g, s0):
                with pe.Fori(0, 2) as q:
                    for t in range(4):
                        up_tile(g, t, q, Count(s0.base + 2 * t, *s0.terms, (8, q)))

            def down_group(g, s0):
                with pe.Fori(0, 4) as q:
                    for t in range(4):
                        down_tile(g, t, q, Count(s0.base + t, *s0.terms, (4, q)), t == 0)

            for t in range(4):
                pe.wait_ge(bank_free[t], 4)
            for j in range(8):
                quad_chunk(Count(C_MLP + j), j, 2 * KT)
            for t in range(4):
                up_tile(0, t, 1, Count(C_MLP + 8 + 2 * t))
            down_group(0, Count(C_MLP + 16))
            with pe.Fori(1, MLP_GROUPS - 1) as g:
                up_group(g, Count(C_MLP, (PER_GROUP, g)))
                down_group(g, Count(C_MLP + 16, (PER_GROUP, g)))
            g = MLP_GROUPS - 1
            s0 = Count(C_MLP + PER_GROUP * g)
            up_group(g, s0)

            def turn_tile(m):
                pe.wait_ge(z_ready, m + 1)
                if m >= 2:
                    pe.wait_ge(tile_ready, m - 1)
                for tb in range(TB):
                    mm = pe.transpose(bank[4 + m % 2][:, tb * P128:(tb + 1) * P128],
                                      hf[:, m % 2, tb * P128:(tb + 1) * P128], ident[:])
                mm.then_inc(z_turned, 1)

            for m in range(KT):
                down_tile(g, m % 4, m // 4, s0 + (16 + m), m == 0)
                if m >= 1:
                    turn_tile(m - 1)
            turn_tile(KT - 1)
            pe.wait_ge(tile_ready, KT - 1)
            token_scale(3)

        @block.scalar
        def _(act):
            def round_w(s):
                r, w = s.place(NRAW), s.place(NW)
                act.wait_ge(raw_landed[r], 16 * s.value(NRAW, 1))
                if s.above(NW):
                    act.wait_ge(chunk_done, s.value(1, 1 - NW))
                nc.scalar.activation(w_hi[:, w], raw[:, r], ACT.Copy).then_inc(hi_ready, 1)

            def spread(n):
                act.wait_ge(spread_done, n)
                nc.scalar.activation(r_all, ps_b[:], ACT.Copy).then_inc(r_all_ready, 1)

            def modulated_hi(n, k, n_scale):
                act.wait_ge(scale_ready, n_scale)
                act.wait_ge(hf_ready, KT * n + k + 1)
                shift = mod1[:, k, 1:2] if n == 0 else modr[:, 1, k:k + 1]
                nc.scalar.activation(act_hi[:, k], hf[:, k % 2], ACT.Identity, bias=shift,
                                     scale=amul[:, n, k:k + 1]).then_inc(act_hi_ready, 1)

            def square_x(m, x_wait):
                act.wait_ge(*x_wait)
                if m % KT >= 2:
                    act.wait_ge(ssq_ready, m - 1)
                nc.scalar.activation(sq[:, m % 2], xy[:, m % KT], ACT.Square).then_inc(sq_ready, 1)

            def take_gate(h, source, s_end):
                act.wait_ge(chunk_done, s_end.value())
                to = xy[:, NRET + h] if isinstance(h, int) else xy[:, bass.ds(h + NRET, 1)].squeeze(1)
                nc.scalar.activation(to, source[:], ACT.Silu).then_inc(gate_ready, 1)

            def take_v(h, s_end):
                act.wait_ge(chunk_done, s_end.value())
                nc.scalar.activation(v_hi[:], bank[2][:], ACT.Copy).then_inc(v_hi_ready, 1)

            def round_rotated(n, to):
                act.wait_ge(rotated, n)
                nc.scalar.activation(to[:], rot_a, ACT.Copy).then_inc(rotated_hi, 1)

            def take_v_tok(hp):
                act.wait_ge(v_turned, hp + 1)
                nc.scalar.activation(v_tok[:].rearrange("p a b -> p (a b)"), ps_d[:], ACT.Copy).then_inc(v_tok_ready, 1)

            def centre_v(hp):
                act.wait_ge(v_turned, hp + 1)
                act.wait_ge(v_mean_ready, hp + 1)
                for tb in range(TB):
                    op = nc.scalar.activation(v_tok[:, tb], ps_d[:, tb * P128:(tb + 1) * P128], ACT.Identity,
                                              bias=v_mean[:, tb:tb + 1])
                op.then_inc(v_tok_ready, 1)

            def take_o(hp):
                act.wait_ge(o_done, hp + 1)
                nc.scalar.activation(sq_hi, ps_a[:], ACT.Square, scale=0.5)
                nc.scalar.activation(sq_head, ps_a[:], ACT.Square, scale=0.5).then_inc(sq_head_ready, 1)
                if not isinstance(hp, int) or hp >= 1:
                    act.wait_ge(y_part_ready, hp)
                nc.scalar.activation(o_sb, ps_a[:], ACT.Copy).then_inc(o_ready, 1)

            def square_o(hp):
                act.wait_ge(o_ready, hp + 1)
                nc.scalar.activation(sq_hi, o_sb, ACT.Square, scale=0.5)
                nc.scalar.activation(sq_head, o_sb, ACT.Square, scale=0.5).then_inc(sq_head_ready, 1)

            def second_term(hp):
                act.wait_ge(r_first_ready, hp - NRET + 1)
                for ib in range(TB):
                    cols = slice(ROWS[ib], ROWS[ib] + (ib + 1) * P128)
                    op = nc.scalar.activation(prob[:, 1, cols], prob[:, 1, cols], ACT.Copy, scale=r_first[:, ib:ib + 1])
                op.then_inc(second_ready, 1)

            def rough_root(hp):
                act.wait_ge(half_ready, 2)
                act.wait_ge(ve_ready, hp + 1)
                nc.scalar.activation(rs0, ve, ACT.Ln, scale=LN_SCALE).then_inc(ln_ready, 1)
                act.wait_ge(ln_ready, hp + 1)
                nc.scalar.activation(rs0, rs0, ACT.Exp, scale=-0.5, bias=ln_shift[:, 0:1]).then_inc(rs0_ready, 1)

            def softmax(hp, blocks, ready, done):
                act.wait_ge(ready, hp - NRET + 1)
                for ib, banks, at in blocks:
                    n = (ib + 1) * P128
                    for comp, acc in enumerate(banks):
                        u = 4 * comp + ib
                        e = nc.scalar.activation(prob[:, comp, ROWS[ib]:ROWS[ib] + n], acc[:, at:at + n], ACT.Exp,
                                                 bias=ntop[:, u:u + 1], scale=QK_SCALE, accum_out=total[:, u:u + 1])
                    if ib == TB - 1:
                        e.then_inc(wide_read, 1)
                e.then_inc(done, 1)

            def softmax1(hp):
                softmax(hp, [(3, (ps_a, ps_b), 0), (2, (ps_c, ps_d), 0)], ntop_ready, prob_ready)

            def softmax2(hp):
                softmax(hp, [(1, (ps_a, ps_b), 0), (0, (ps_a, ps_b), 256)], ntop2_ready, prob2_ready)
                second_term(hp)

            ret_stage = {1: centre_v, 2: take_o, 4: rough_root}
            dif_stage = {0: softmax1, 1: softmax2, 2: take_v_tok, 4: square_o, 5: rough_root}

            def head(h, s0, slots, stage):
                for j in range(slots):
                    round_w(s0 + (j + 1))
                    if j == 0:
                        take_v(h - 1, s0)
                    if j in stage:
                        stage[j](h - 1)
                    if j == 2:
                        round_rotated(2 * h + 1, q_hi)
                    if j == 4:
                        round_rotated(2 * h + 2, k_hi)
                if slots == 8:
                    take_gate(h, bank[3], s0 + 8)

            act.dma_start(vec[:], vecs).then_inc(vec_landed, 16)
            act.dma_start(ident[:], ident_in).then_inc(ident_landed, 16)
            act.dma_start(lam_in, lams.partition_broadcast(P128)).then_inc(lam_landed, 16)
            act.dma_start(mask_f, mask_in).then_inc(mask_landed, 16)
            act.wait_ge(c_landed, 16)
            nc.scalar.activation(silu_c[:], silu_c[:], ACT.Silu).then_inc(silu_ready, 1)
            for m in range(KT):
                square_x(m, (x_landed[m // 2], 16))
            act.dma_start(rot_sb[:, 0], rot[0, 0]).then_inc(rot_landed, 16)
            act.dma_start(rot_sb[:, 1], rot[0, 1]).then_inc(rot_landed, 16)
            act.dma_start(decay_sb[:], decay[0]).then_inc(decay_landed, 16)
            round_w(Count(0))
            spread(1)
            modulated_hi(0, 0, 1)
            modulated_hi(0, 1, 1)
            for p in range(KT // 2):
                round_w(Count(2 * p + 1))
                round_w(Count(2 * p + 2))
                if p < KT // 2 - 1:
                    modulated_hi(0, 2 * p + 2, p + 2)
                    modulated_hi(0, 2 * p + 3, p + 2)
                if p == 4:
                    act.wait_ge(lam_dotted, 1)
                    nc.scalar.activation(lam_exp[:], lam_sum[:], ACT.Exp).then_inc(lam_exped, 1)
            round_rotated(1, q_hi)
            for h in range(2):
                take_gate(h, bank[3 + h], Count(FIRST))
            round_rotated(2, k_hi)
            for h in range(2, EARLY + 1):
                take_gate(h, bank[3 + h], Count(FIRST))
            for h in range(1, EARLY + 1):
                head(h, Count(FIRST + 6 * (h - 1)), 6, ret_stage)
            with act.Fori(EARLY + 1, NRET) as h:
                head(h, Count(C_DIF - 8 * NRET, (8, h)), 8, ret_stage)
            head(NRET, Count(C_DIF), 6, ret_stage)
            head(NRET + 1, Count(C_DIF + 6), 6, dif_stage)
            with act.Fori(0, 3) as i:
                for e in range(2):
                    head(2 * i + (NRET + 2 + e), Count(C_DIF + 12 + 6 * e, (12, i)), 6, dif_stage)

            def split_y(k):
                if k < NRET:
                    act.wait_ge(y_ret_ready, k + 1)
                else:
                    act.wait_ge(y_dif_ready, k - NRET + 1)
                nc.scalar.activation(act_hi[:, k], xy[:, k], ACT.Copy).then_inc(act_hi_ready, 1)

            take_v(NRET + NDIF - 1, Count(C_OUT))
            split_y(0)
            split_y(1)
            for j in range(8):
                if j < 7:
                    round_w(Count(C_OUT + j + 1))
                    if j == 6:
                        round_w(Count(C_OUT + 8))
                    for k in Y_SPLITS[j]:
                        split_y(k)
                if j in dif_stage:
                    dif_stage[j](NRET + NDIF - 1)
            round_w(Count(C_OUT + 9))
            for m in range(4):
                square_x(KT + m, (bank_free[m % 4], m // 4 + 1))
            for g in range(1, 4):
                for t in range(4):
                    for half in range(2 if (g, t) != (1, 0) else 1):
                        round_w(Count(C_OUT + 8 * g + 2 * t + half + (1 if (g, t) != (1, 0) else 2)))
                    m = 4 * g + t
                    square_x(KT + m, (bank_free[m % 4], m // 4 + 1))
            spread(2)
            modulated_hi(1, 0, 9)
            modulated_hi(1, 1, 9)
            for j in range(8):
                if j < 7:
                    modulated_hi(1, 2 * j + 2, 9)
                    modulated_hi(1, 2 * j + 3, 9)
                round_w(Count(C_MLP + j + 1))

            def take_u(g, i, t, s_end):
                n = 8 * g + i
                act.wait_ge(chunk_done, s_end.value())
                if not isinstance(n, int) or n >= 2:
                    act.wait_ge(u_ready, n - 1)
                nc.scalar.activation(relu[:, t % 2], bank[t][:], ACT.Relu).then_inc(relu_ready, 1)
                act.wait_ge(relu_ready, n + 1)
                nc.scalar.activation(u_hi[:, i], relu[:, t % 2], ACT.Square).then_inc(u_hi_ready, 1)

            def up_quad(g, q, s0):
                for t in range(4):
                    for half in range(2):
                        round_w(s0 + (2 * t + half + 1))
                    take_u(g, 4 * q + t, t, s0 + (2 * t + 2))

            def down_group(s0):
                with act.Fori(0, 4) as q:
                    for t in range(4):
                        round_w(Count(s0.base + t + 1, *s0.terms, (4, q)))

            for t in range(4):
                take_u(0, t, t, Count(C_MLP + 8))
            up_quad(0, 1, Count(C_MLP + 8))
            down_group(Count(C_MLP + 16))
            with act.Fori(1, MLP_GROUPS - 1) as g:
                with act.Fori(0, 2) as q:
                    up_quad(g, q, Count(C_MLP, (PER_GROUP, g), (8, q)))
                down_group(Count(C_MLP + 16, (PER_GROUP, g)))
            g = MLP_GROUPS - 1
            s0 = C_MLP + PER_GROUP * g
            with act.Fori(0, 2) as q:
                up_quad(g, q, Count(s0, (8, q)))
            for m in range(KT):
                if m < KT - 1:
                    round_w(Count(s0 + 17 + m))
                square_x(2 * KT + m, (bank_free[m % 4], 4 + 4 * g + m // 4 + 1))
                if m >= 2:
                    act.wait_ge(z_turned, m - 1)
                nc.scalar.activation(hf[:, m % 2], xy[:, m], ACT.Copy,
                                     scale=vec[:, V_FIN + m:V_FIN + m + 1]).then_inc(z_ready, 1)
            act.wait_ge(tok_r_ready, 3)
            act.wait_ge(tile_ready, KT)
            last = xy[:, :, 3 * P128:]
            nc.scalar.activation(last, last, ACT.Copy, scale=tok_r[:, 3:4]).then_inc(scaled_s, 1)

        @block.vector
        def _(dve):
            def rest_w(s):
                r, w = s.place(NRAW), s.place(NW)
                dve.wait_ge(hi_ready, s.value(1, 1))
                nc.vector.tensor_tensor(w_lo[:, w], raw[:, r], w_hi[:, w].bitcast(F32), ALU.subtract).then_inc(lo_ready, 1)

            def dot_ada(a, to):
                r, landed = ada_place(a)
                dve.wait_ge(ada_landed[r], 16 * landed)
                half = a.base % 2
                nc.vector.tensor_tensor_reduce(ada_at(r), ada_at(r), silu_c[:, half * HALF:(half + 1) * HALF],
                                               1.0, 0.0, ALU.mult, ALU.add, to).then_inc(dot_done, 1)

            def modulation1(p):
                for k in range(2 * p, 2 * p + 2):
                    for e in range(4):
                        dot_ada(Count(4 * k + e), part1[:, k, e // 2, e % 2:e % 2 + 1])
                ks = slice(2 * p, 2 * p + 2)
                dve.wait_ge(dot_done, 8 * p + 8)
                nc.vector.tensor_tensor(sum1[:], part1[:, ks, :, 0], part1[:, ks, :, 1], ALU.add).then_inc(mod_summed, 1)
                dve.wait_ge(mod_summed, p + 1)
                bias = vec[:, V_B1 + 4 * p:V_B1 + 4 * p + 4].rearrange("p (a b) -> p a b", b=2)
                nc.vector.tensor_tensor(mod1[:, ks], sum1[:], bias, ALU.add).then_inc(mod_ready, 1)
                dve.wait_ge(mod_ready, p + 1)
                nc.vector.scalar_tensor_tensor(amul[:, 0, ks], mod1[:, ks, 0], 1.0,
                                               vec[:, V_N1 + 2 * p:V_N1 + 2 * p + 2], ALU.add, ALU.mult)\
                    .then_inc(scale_ready, 1)

            def token_scale(n):
                dve.wait_ge(mean_done, n)
                nc.vector.tensor_scalar(tok_v[:], ps_a[:, 0:TB], NORM_EPS, None, ALU.add).then_inc(tok_v_ready, 1)
                dve.wait_ge(tok_r_ready, n)
                if n < 3:
                    nc.vector.tensor_tensor(diag.rearrange("p (a b) -> p a b", a=TB),
                                            ident[:].unsqueeze(1).broadcast_to([P128, TB, P128]),
                                            tok_r[:].unsqueeze(2).broadcast_to([P128, TB, P128]), ALU.mult)\
                        .then_inc(diag_ready, 1)

            def modulated_rest(n, k):
                dve.wait_ge(scale_ready, k // 2 + 1 if n == 0 else KT // 2 + 1)
                dve.wait_ge(hf_ready, KT * n + k + 1)
                shift = mod1[:, k, 1:2] if n == 0 else modr[:, 1, k:k + 1]
                nc.vector.tensor_scalar(hm[:, k % 2], hf[:, k % 2], amul[:, n, k:k + 1], shift, ALU.mult, ALU.add)\
                    .then_inc(hm_ready, 1)
                dve.wait_ge(hm_ready, KT * n + k + 1)
                dve.wait_ge(act_hi_ready, 2 * KT * n + k + 1)
                nc.vector.tensor_tensor(act_lo[:, k], hm[:, k % 2], act_hi[:, k].bitcast(F32), ALU.subtract)\
                    .then_inc(act_ready, 1)

            def sum_square(m):
                dve.wait_ge(sq_ready, m + 1)
                if m % KT:
                    dve.wait_ge(ssq_ready, m)
                    nc.vector.tensor_tensor(ssq, ssq, sq[:, m % 2], ALU.add).then_inc(ssq_ready, 1)
                else:
                    nc.vector.tensor_copy(ssq, sq[:, m % 2]).then_inc(ssq_ready, 1)

            def rotate(h, src, s_end, read, is_k, dif):
                n = 2 * h + is_k
                dve.wait_ge(chunk_done, s_end.value())
                if is_k:
                    dve.wait_ge(q_ready, h + 1)
                if not isinstance(h, int) or h > 0:
                    dve.wait_ge(v_turned, h)
                    if not is_k:
                        dve.wait_ge(k_ready, h)
                dve.wait_ge(rot_landed, 64 if dif else 32)
                cos, sin = rot_sb[:, 0], rot_sb[:, 1]
                nc.vector.tensor_tensor(rot_a, src[:], cos, ALU.mult)
                if dif:
                    nc.vector.stream_shuffle(rot_b, src[:], [(i + 8) % 16 if i < 16 else i for i in range(32)])\
                        .then_inc(read, 1)
                    dve.wait_ge(read, h + 1)
                    nc.vector.tensor_tensor(rot_b, rot_b, sin, ALU.mult).then_inc(turned, 1)
                    dve.wait_ge(turned, n - 2 * NRET + 1)
                else:
                    nc.vector.tensor_tensor(rot_b[0:64], src[64:128], sin[64:128], ALU.mult)
                    nc.vector.tensor_tensor(rot_b[64:128], src[0:64], sin[0:64], ALU.mult).then_inc(read, 1)
                    dve.wait_ge(read, h + 1)
                nc.vector.tensor_tensor(rot_a, rot_a, rot_b, ALU.add).then_inc(rotated, 1)

            def rotate_q(h, s_end, dif):
                rotate(h, bank[0], s_end, q_read, 0, dif)

            def rotate_k(h, s_end, dif):
                rotate(h, bank[1], s_end, k_read, 1, dif)

            def decay_strips(hp):
                dve.wait_ge(scores_done, hp + 1)
                dve.wait_ge(decay_landed, 16 * hp + 16)
                for jb, (acc, at) in enumerate([(ps_a, 0), (ps_b, 0), (ps_c, 0), (ps_c, 256)]):
                    n = TOK - jb * P128
                    op = nc.vector.tensor_tensor(strips[:, STRIP[jb]:STRIP[jb] + n], acc[:, at:at + n],
                                                 decay_sb[:, 0:n], ALU.mult)
                op.then_inc(strips_ready, 1)

            def rest_v(hp):
                dve.wait_ge(v_hi_ready, hp + 1)
                nc.vector.tensor_tensor(v_lo[:], bank[2][:], v_hi[:].bitcast(F32), ALU.subtract).then_inc(v_ready, 1)

            def means_of_v(hp):
                dve.wait_ge(v_turned, hp + 1)
                nc.vector.reduce_sum(v_sum[:], ps_d[:].rearrange("p (a b) -> p a b", a=TB), AX_X).then_inc(v_summed, 1)
                dve.wait_ge(v_summed, hp + 1)
                nc.vector.tensor_scalar(v_mean[:], v_sum[:], -1.0 / HD, None, ALU.mult).then_inc(v_mean_ready, 1)

            def var_eps(hp):
                dve.wait_ge(var_done, hp + 1)
                nc.vector.tensor_scalar(ve, ps_c[:], 4.0, GN_EPS, ALU.mult, ALU.add).then_inc(ve_ready, 1)

            def finish_ret(hp):
                dve.wait_ge(rs_ready, hp + 1)
                dve.wait_ge(gate_ready, hp + 1)
                if isinstance(hp, int):
                    weight, to, gate = vec[:, V_HEAD + hp:V_HEAD + hp + 1], xy[:, hp], xy[:, NRET + hp]
                else:
                    weight = vec[:, bass.ds(hp + V_HEAD, 1)]
                    to, gate = xy[:, bass.ds(hp, 1)].squeeze(1), xy[:, bass.ds(hp + NRET, 1)].squeeze(1)
                nc.vector.scalar_tensor_tensor(to, o_sb, weight, rs1, ALU.mult, ALU.mult).then_inc(y_part_ready, 1)
                dve.wait_ge(y_part_ready, hp + 1)
                nc.vector.tensor_tensor(to, to, gate, ALU.mult).then_inc(y_ret_ready, 1)

            def clamp_o(hp):
                dve.wait_ge(o_done, hp + 1)
                nc.vector.tensor_scalar(o_sb, ps_a[:], SQUARE_TOP, -SQUARE_TOP, ALU.min, ALU.max).then_inc(o_ready, 1)

            def finish_dif(hp):
                dve.wait_ge(rs_ready, hp + 1)
                nc.vector.scalar_tensor_tensor(rs1, ve, MEAN_TOP, rs1, ALU.is_lt, ALU.mult).then_inc(root_gated, 1)
                dve.wait_ge(root_gated, hp - NRET + 1)
                weight = vec[:, V_HEAD + hp:V_HEAD + hp + 1] if isinstance(hp, int) else vec[:, bass.ds(hp + V_HEAD, 1)]
                to = xy[:, hp] if isinstance(hp, int) else xy[:, bass.ds(hp, 1)].squeeze(1)
                nc.vector.scalar_tensor_tensor(to, o_sb, weight, rs1, ALU.mult, ALU.mult).then_inc(y_dif_ready, 1)

            def row_tops(hp, blocks, scores, found, ready):
                dve.wait_ge(scores, hp + 1 if scores is scores_done else hp - NRET + 1)
                for ib, banks, at in blocks:
                    n = (ib + 1) * P128
                    for comp, acc in enumerate(banks):
                        op = nc.vector.reduce_max(top[:, 4 * comp + ib:4 * comp + ib + 1], acc[:, at:at + n], AX_X)
                op.then_inc(found, 1)
                dve.wait_ge(found, hp - NRET + 1)
                first = blocks[-1][0]
                cols = [t[:].rearrange("p (a b) -> p a b", a=2)[:, :, first:first + 2] for t in (ntop, top)]
                nc.vector.tensor_scalar(cols[0], cols[1], -QK_SCALE, None, ALU.mult).then_inc(ready, 1)

            def tops1(hp):
                row_tops(hp, [(3, (ps_a, ps_b), 0), (2, (ps_c, ps_d), 0)], scores_done, top_ready, ntop_ready)

            def tops2(hp):
                row_tops(hp, [(1, (ps_a, ps_b), 0), (0, (ps_a, ps_b), 256)], scores2_done, top2_ready, ntop2_ready)

            def factors(hp):
                n = hp - NRET + 1
                dve.wait_ge(prob2_ready, n)
                nc.vector.reciprocal(rtotal[:], total[:]).then_inc(rtotal_ready, 1)
                dve.wait_ge(rtotal_ready, n)
                dve.wait_ge(lam_ready, 1)
                nc.vector.tensor_scalar(r_first[:], rtotal[:, 4:8], neg_lam[:, 0:1], None, ALU.mult).then_inc(r_first_ready, 1)

            def combine(hp):
                dve.wait_ge(second_ready, hp - NRET + 1)
                for ib in range(TB):
                    cols = slice(ROWS[ib], ROWS[ib] + (ib + 1) * P128)
                    op = nc.vector.scalar_tensor_tensor(prob[:, 0, cols], prob[:, 0, cols], rtotal[:, ib:ib + 1],
                                                        prob[:, 1, cols], ALU.mult, ALU.add)
                op.then_inc(diff_ready, 1)

            def diff_strips(hp):
                dve.wait_ge(diff_turned, hp - NRET + 1)
                for acc, at, n in ((ps_a, STRIP[0], 512), (ps_b, STRIP[1], 384), (ps_c, STRIP[2], 384)):
                    op = nc.vector.tensor_copy(strips[:, at:at + n], acc[:, 0:n])
                op.then_inc(strips_ready, 1)

            def modulation_rest(a, part):
                for e in range(2):
                    dot_ada(a + e, partr[:, part, e:e + 1])

            def modulation_sum(n, col):
                dve.wait_ge(dot_done, 16 * n + A_RET)
                nc.vector.tensor_tensor(sumr[:], partr[:, :, 0], partr[:, :, 1], ALU.add).then_inc(modr_summed, 1)
                dve.wait_ge(modr_summed, n)
                flat = modr[:].rearrange("p a b -> p (a b)")
                to = flat[:, bass.ds(col, 8)] if not isinstance(col, int) else flat[:, col:col + 8]
                bias = vec[:, bass.ds(col + V_B, 8)] if not isinstance(col, int) else vec[:, V_B + col:V_B + col + 8]
                nc.vector.tensor_tensor(to, sumr[:], bias, ALU.add).then_inc(modr_ready, 1)

            def head_ret(h, s0, slots, dif=False):
                part = 0
                for j in range(len(slots)):
                    if j == 1:
                        means_of_v(h - 1)
                    rest_w(s0 + (j + 1))
                    if j == 0:
                        rest_v(h - 1)
                    if j == 1:
                        if not isinstance(h, int) or h > 1:
                            finish_ret(h - 2)
                    if j == 2:
                        rotate_q(h, s0 + 2, dif)
                    if j == 4:
                        var_eps(h - 1)
                        rotate_k(h, s0 + 4, dif)
                    for _ in range(slots[j]):
                        a = Count(A_RET - 16 + 16 * h + 2 * part) if isinstance(h, int) else \
                            Count(A_RET - 16 + 2 * part, (16, h))
                        modulation_rest(a, part)
                        part += 1
                    if j == 0:
                        decay_strips(h - 1)
                modulation_sum(h, 8 * h - 8)

            def head_dif(h, s0):
                for j in range(6):
                    if j == 3:
                        diff_strips(h - 1)
                    rest_w(s0 + (j + 1))
                    if j == 0:
                        tops1(h - 1)
                        rest_v(h - 1)
                    if j == 1:
                        tops2(h - 1)
                        if isinstance(h, int) and h == NRET + 1:
                            finish_ret(h - 2)
                        else:
                            finish_dif(h - 2)
                        factors(h - 1)
                    if j == 2:
                        combine(h - 1)
                        rotate_q(h, s0 + 2, True)
                    if j == 4:
                        clamp_o(h - 1)
                        rotate_k(h, s0 + 4, True)
                    if j == 5:
                        var_eps(h - 1)

            nc.vector.memset(ones[:], 1.0).then_inc(const_ready, 1)
            nc.vector.memset(inv_d[:], 1.0 / D).then_inc(const_ready, 1)
            dve.wait_ge(const_ready, 1)
            nc.vector.tensor_scalar(inv_hd[:], ones[:], 1.0 / HD, None, ALU.mult).then_inc(const_ready, 1)
            dve.wait_ge(ident_landed, 16)
            dve.wait_ge(mask_landed, 16)
            nc.vector.tensor_copy(ident_r[:], ident[:])
            nc.vector.tensor_copy(ident_b[:], ident[:]).then_inc(const_ready, 1)
            nc.vector.tensor_copy(mask[:], mask_f).then_inc(setup_ready, 1)
            for m in range(KT):
                sum_square(m)
            token_scale(1)
            dve.wait_ge(vec_landed, 16)
            dve.wait_ge(silu_ready, 1)
            modulation1(0)
            modulated_rest(0, 0)
            modulated_rest(0, 1)
            for p in range(KT // 2):
                if p < KT // 2 - 1:
                    modulation1(p + 1)
                    modulated_rest(0, 2 * p + 2)
                    modulated_rest(0, 2 * p + 3)
                if p == 3:
                    dve.wait_ge(lam_landed, 16)
                    for e in range(2):
                        op = nc.vector.tensor_tensor_reduce(lam_prod[:, e], lam_in[:, 2 * e], lam_in[:, 2 * e + 1], 1.0, 0.0,
                                                            ALU.mult, ALU.add, lam_sum[:, e:e + 1])
                    op.then_inc(lam_dotted, 1)
                    dif_w = vec[:, V_HEAD + NRET:V_HEAD + NRET + NDIF]
                    nc.vector.tensor_scalar(dif_w, dif_w, 1.0 - LAM_INIT, None, ALU.mult).then_inc(setup_ready, 1)
            dve.wait_ge(lam_exped, 1)
            nc.vector.tensor_scalar(neg_lam[:], lam_exp[:, 1:2], lam_exp[:, 0:1], LAM_INIT, ALU.subtract, ALU.subtract)\
                .then_inc(lam_ready, 1)
            rotate_q(0, Count(FIRST), False)
            rotate_k(0, Count(FIRST), False)
            dve.wait_ge(lo_ready, FIRST + 1)
            for h in range(1, EARLY + 1):
                head_ret(h, Count(FIRST + 6 * (h - 1)), ADA_6)
            with dve.Fori(EARLY + 1, NRET) as h:
                head_ret(h, Count(C_DIF - 8 * NRET, (8, h)), ADA_8)
            head_ret(NRET, Count(C_DIF), ADA_6, dif=True)
            dve.wait_ge(modr_ready, NRET)
            nc.vector.scalar_tensor_tensor(amul[:, 1], modr[:, 2], 1.0, vec[:, V_N2:V_N2 + KT], ALU.add, ALU.mult)\
                .then_inc(scale_ready, 1)
            head_dif(NRET + 1, Count(C_DIF + 6))
            with dve.Fori(0, 3) as i:
                for e in range(2):
                    head_dif(2 * i + (NRET + 2 + e), Count(C_DIF + 12 + 6 * e, (12, i)))

            def split_y(k):
                dve.wait_ge(act_hi_ready, KT + k + 1)
                nc.vector.tensor_tensor(act_lo[:, k], xy[:, k], act_hi[:, k].bitcast(F32), ALU.subtract).then_inc(act_ready, 1)

            rest_v(NRET + NDIF - 1)
            split_y(0)
            split_y(1)
            hp = NRET + NDIF - 1
            for j in range(8):
                if j < 7:
                    rest_w(Count(C_OUT + j + 1))
                if j == 0:
                    tops1(hp)
                if j == 1:
                    tops2(hp)
                    finish_dif(hp - 1)
                    factors(hp)
                if j == 2:
                    combine(hp)
                if j == 3:
                    diff_strips(hp)
                if j == 4:
                    clamp_o(hp)
                if j == 5:
                    var_eps(hp)
                if j == 6:
                    finish_dif(hp)
                if j < 7:
                    if j == 6:
                        rest_w(Count(C_OUT + 8))
                    for k in Y_SPLITS[j]:
                        split_y(k)

            def residual(part, m, t, s_end):
                dve.wait_ge(chunk_done, s_end.value())
                if isinstance(m, int):
                    to, gate_col = xy[:, m], modr[:, part, m:m + 1]
                else:
                    to, gate_col = xy[:, bass.ds(m, 1)].squeeze(1), modr[:, part, bass.ds(m, 1)]
                nc.vector.scalar_tensor_tensor(to, bank[t][:], gate_col, to, ALU.mult, ALU.add).then_inc(bank_free[t], 1)

            def residual_out(m, s_end):
                dve.wait_ge(x_landed[m // 2], 32)
                residual(0, m, m % 4, s_end)

            for m in range(4):
                residual_out(m, Count(C_OUT + 8))
                if m == 0:
                    rest_w(Count(C_OUT + 9))
                sum_square(KT + m)
            for g in range(1, 4):
                for t in range(4):
                    for half in range(2 if (g, t) != (1, 0) else 1):
                        rest_w(Count(C_OUT + 8 * g + 2 * t + half + (1 if (g, t) != (1, 0) else 2)))
                    m = 4 * g + t
                    residual_out(m, Count(C_OUT + 2 * m + 2))
                    sum_square(KT + m)
            token_scale(2)
            modulated_rest(1, 0)
            modulated_rest(1, 1)
            for j in range(8):
                if j < 7:
                    modulated_rest(1, 2 * j + 2)
                    modulated_rest(1, 2 * j + 3)
                rest_w(Count(C_MLP + j + 1))

            def rest_u(g, i, t):
                n = 8 * g + i
                dve.wait_ge(relu_ready, n + 1)
                nc.vector.tensor_tensor(usq[:, t % 2], relu[:, t % 2], relu[:, t % 2], ALU.mult).then_inc(usq_ready, 1)
                dve.wait_ge(usq_ready, n + 1)
                dve.wait_ge(u_hi_ready, n + 1)
                nc.vector.tensor_tensor(u_lo[:, i], usq[:, t % 2], u_hi[:, i].bitcast(F32), ALU.subtract).then_inc(u_ready, 1)

            def up_quad(g, q, s0):
                for t in range(4):
                    for half in range(2):
                        rest_w(s0 + (2 * t + half + 1))
                    rest_u(g, 4 * q + t, t)

            def down_group(s0):
                with dve.Fori(0, 4) as q:
                    for t in range(4):
                        done = Count(s0.base + t + 1, *s0.terms, (4, q))
                        rest_w(done)
                        residual(3, 4 * q + t, t, done)

            for t in range(4):
                rest_u(0, t, t)
            up_quad(0, 1, Count(C_MLP + 8))
            down_group(Count(C_MLP + 16))
            with dve.Fori(1, MLP_GROUPS - 1) as g:
                with dve.Fori(0, 2) as q:
                    up_quad(g, q, Count(C_MLP, (PER_GROUP, g), (8, q)))
                down_group(Count(C_MLP + 16, (PER_GROUP, g)))
            g = MLP_GROUPS - 1
            s0 = C_MLP + PER_GROUP * g
            with dve.Fori(0, 2) as q:
                up_quad(g, q, Count(s0, (8, q)))

            def take_tile(m):
                dve.wait_ge(z_turned, m + 1)
                nc.vector.tensor_copy(xy[:, m], bank[4 + m % 2][:]).then_inc(tile_ready, 1)

            for m in range(KT):
                if m < KT - 1:
                    rest_w(Count(s0 + 17 + m))
                residual(3, m, m % 4, Count(s0 + 17 + m))
                if m >= 1:
                    take_tile(m - 1)
                sum_square(2 * KT + m)
            take_tile(KT - 1)
            token_scale(3)
            dve.wait_ge(tile_ready, KT)
            for tb in range(3):
                tile = xy[:, :, tb * P128:(tb + 1) * P128]
                nc.vector.tensor_scalar(tile, tile, tok_r[:, tb:tb + 1], None, ALU.mult).then_inc(scaled_v, 1)

        @block.gpsimd
        def _(pool):
            def normed(n, k):
                pool.wait_ge(r_all_ready, n + 1)
                if KT * n + k >= 2:
                    pool.wait_ge(hm_ready, KT * n + k - 1)
                    if k >= 2:
                        pool.wait_ge(act_hi_ready, 2 * KT * n + k - 1)
                nc.gpsimd.tensor_tensor(hf[:, k % 2], xy[:, k], r_all, ALU.mult).then_inc(hf_ready, 1)

            def rest_w(s):
                pool.wait_ge(hi_ready, s + 1)
                nc.gpsimd.tensor_tensor(w_lo[:, s % NW], raw[:, s % NRAW], w_hi[:, s % NW].bitcast(F32), ALU.subtract)\
                    .then_inc(lo_ready, 1)

            def token_root(n):
                pool.wait_ge(tok_v_ready, n)
                nc.gpsimd.tensor_tensor(tok_r[:], tok_v[:], minus_half[:], ALU.pow).then_inc(tok_r_ready, 1)

            def rest_rotated(n, to_hi, to_lo, ready):
                pool.wait_ge(rotated_hi, n)
                nc.gpsimd.tensor_tensor(to_lo[:], rot_a, to_hi[:].bitcast(F32), ALU.subtract).then_inc(ready, 1)

            def rest_q(h):
                rest_rotated(2 * h + 1, q_hi, q_lo, q_ready)

            def rest_k(h):
                rest_rotated(2 * h + 2, k_hi, k_lo, k_ready)

            def square_rest(hp):
                pool.wait_ge(sq_head_ready, hp + 1)
                nc.gpsimd.tensor_tensor(sq_lo, sq_head, sq_hi.bitcast(F32), ALU.subtract).then_inc(sq_lo_ready, 1)

            def refine_root(hp):
                pool.wait_ge(rs0_ready, hp + 1)
                nc.gpsimd.tensor_tensor(rs1, ve, rs0, ALU.mult).then_inc(newton, 1)
                pool.wait_ge(newton, 3 * hp + 1)
                nc.gpsimd.tensor_tensor(rs1, rs1, rs0, ALU.mult).then_inc(newton, 1)
                pool.wait_ge(newton, 3 * hp + 2)
                nc.gpsimd.tensor_scalar(rs1, rs1, -0.5, 1.5, ALU.mult, ALU.add).then_inc(newton, 1)
                pool.wait_ge(newton, 3 * hp + 3)
                nc.gpsimd.tensor_tensor(rs1, rs1, rs0, ALU.mult).then_inc(rs_ready, 1)

            nc.gpsimd.memset(ln_shift[:], 0.5 * float(np.log(LN_SCALE))).then_inc(half_ready, 1)
            nc.gpsimd.memset(minus_half[:], -0.5).then_inc(half_ready, 1)
            pool.wait_ge(half_ready, 2)
            rest_w(0)
            token_root(1)
            normed(0, 0)
            normed(0, 1)
            for p in range(KT // 2):
                rest_w(2 * p + 1)
                if p < KT // 2 - 1:
                    normed(0, 2 * p + 2)
                    normed(0, 2 * p + 3)
                    rest_w(2 * p + 2)
            rest_w(FIRST)
            rest_q(0)
            rest_k(0)
            for h in range(1, NRET + 1):
                rest_q(h)
                square_rest(h - 1)
                rest_k(h)
                refine_root(h - 1)
            for h in range(NRET + 1, NRET + NDIF):
                rest_q(h)
                square_rest(h - 1)
                rest_k(h)
                refine_root(h - 1)
            square_rest(NRET + NDIF - 1)
            refine_root(NRET + NDIF - 1)
            token_root(2)
            for k in range(KT):
                normed(1, k)
            token_root(3)


def blocks_of(w):
    k, m = w.shape
    return w.reshape(k // P128, P128, m // P128, P128).transpose(0, 2, 1, 3)


def tile_chunks(blocks, ms):
    n_k = blocks.shape[0]
    b = blocks[:, ms].reshape(n_k // BLOCKS, BLOCKS, len(ms), P128, P128)
    return b.transpose(2, 0, 3, 1, 4).reshape(-1, P128, CHUNK)


def first_chunks(blocks, ms):
    return blocks[:, ms].transpose(0, 2, 1, 3).reshape(-1, P128, CHUNK)


def quad_chunks(blocks, ms):
    b = blocks[:, ms].reshape(8, 2, 4, P128, P128)
    return b.transpose(0, 3, 1, 2, 4).reshape(-1, P128, CHUNK)


def weight_chunks(w_in, w_out, w1, w2):
    b_in, b_out, b_up, b_down = (blocks_of(w) for w in (w_in, w_out, w1, w2))
    first = [0, NRET, 2 * NRET] + [3 * NRET + h for h in range(EARLY + 1)]
    order = [[h, NRET + h, 2 * NRET + h] + ([3 * NRET + h] if h > EARLY else []) for h in range(1, NRET)]
    order += [[4 * NRET + d, 4 * NRET + NDIF + d, 4 * NRET + 2 * NDIF + d] for d in range(NDIF)]
    parts = [first_chunks(b_in, first)] + [tile_chunks(b_in, ms) for ms in order]
    parts += [quad_chunks(b_out, [0, 1, 2, 3]), tile_chunks(b_out, list(range(4, KT)))]
    for g in range(MLP_GROUPS):
        ms = list(range(BLOCKS * g, BLOCKS * g + BLOCKS))
        parts += [quad_chunks(b_up, ms[:4]), tile_chunks(b_up, ms[4:])] if g == 0 else [tile_chunks(b_up, ms)]
        parts.append(tile_chunks(b_down[ms], list(range(KT))))
    return np.concatenate(parts)


def ada_rows(w_ada):
    cols = w_ada.T.reshape(6, KT, P128, 2, HALF).transpose(0, 1, 3, 2, 4)
    first = np.stack([cols[1], cols[0]], axis=1).reshape(-1, P128, HALF)
    rest = np.stack([cols[2], cols[3], cols[4], cols[5]]).reshape(-1, P128, HALF)
    return np.concatenate([first, rest])


def columns(v):
    return v.reshape(-1, P128).T


def packed_vectors(b_ada, norm1_w, norm2_w, final_norm_w, ret_gn_w, diff_subln_w):
    b = b_ada.reshape(6, KT, P128)
    b1 = np.stack([b[1], b[0]], axis=1).reshape(-1)
    rest = np.concatenate([b[2], b[3], b[4], b[5]]).reshape(-1)
    return np.concatenate([columns(v) for v in (b1, rest, norm1_w, norm2_w, final_norm_w, ret_gn_w, diff_subln_w)],
                          axis=1)


def rotary_tables():
    f = np.float32
    pos = np.arange(TOK, dtype=f)
    out = np.zeros((2, 2, P128, TOK), f)
    inv = f(10000.0) ** (-np.arange(0, HD, 2, dtype=f) / f(HD))
    ang = inv[:, None] * pos[None, :]
    out[0, 0] = np.tile(np.cos(ang), (2, 1))
    out[0, 1] = np.concatenate([np.sin(ang), -np.sin(ang)])
    rot_dim = DQK // 4
    inv = f(500000.0) ** (-np.arange(0, rot_dim, 2, dtype=f) / f(rot_dim))
    ang = inv[:, None] * pos[None, :]
    out[1, 0] = 1.0
    for at in (0, DQK):
        out[1, 0, at:at + rot_dim] = np.tile(np.cos(ang), (2, 1))
        out[1, 1, at:at + rot_dim] = np.concatenate([-np.sin(ang), np.sin(ang)])
    return out


def decay_tables():
    lg = np.log(np.float32(1.0) - np.float32(2.0) ** (np.float32(-5.0) - np.arange(NRET, dtype=np.float32)))
    rel = np.arange(TOK)[None, :] - np.arange(P128)[:, None]
    d = np.exp(np.maximum(rel, 0)[None] * lg.astype(np.float64)[:, None, None]) * float(HD) ** -0.5
    return np.where(rel[None] >= 0, d, 0.0).astype(np.float32)


def kernel(x, c, w_ada, b_ada, norm1_w, norm2_w, w_in, ret_gn_w, diff_lq1, diff_lk1, diff_lq2, diff_lk2,
           diff_subln_w, w_out, w_mlp1, w_mlp2, final_norm_w):
    import concourse.bacc as bacc
    from concourse.bass_utils import run_bass_kernel_spmd

    rows = np.arange(P128)
    arrays = {
        "x_t": x[0].T.reshape(KT, P128, TOK).transpose(1, 0, 2),
        "c_row": c[0],
        "ada": ada_rows(w_ada[0]),
        "weights": weight_chunks(w_in[0], w_out[0], w_mlp1[0], w_mlp2[0]),
        "vecs": packed_vectors(b_ada[0], norm1_w[0], norm2_w[0], final_norm_w, ret_gn_w[0], diff_subln_w[0]),
        "lams": np.stack([diff_lq1[0], diff_lk1[0], diff_lq2[0], diff_lk2[0]]),
        "rot": rotary_tables(),
        "decay": decay_tables(),
        "ident_in": np.eye(P128, dtype=np.float32),
        "mask_in": np.where(rows[None, :] <= rows[:, None], 0.0, -1e30).astype(np.float32),
    }
    arrays = {name: np.ascontiguousarray(a) for name, a in arrays.items()}
    nc = bacc.Bacc("TRN2", target_bir_lowering=False, num_devices=1)
    aps = [nc.dram_tensor(name, a.shape, mybir.dt.from_np(a.dtype), kind="ExternalInput").ap()
           for name, a in arrays.items()]
    out = nc.dram_tensor("out", (TOK, D), F32, kind="ExternalOutput").ap()
    block_kernel(nc, *aps, out)
    r = run_bass_kernel_spmd(nc, [arrays], core_ids=[0])
    return r.results[0]["out"].reshape(1, TOK, D)
```
